# Optimizing a Trainium2 kernel written in Bass

```python
import jax
import jax.numpy as jnp
from jax import lax
import numpy as np

D_MODEL = 1024
BATCH = 1
SEQ = 2048
DEPTH = 1
DEC_BATCH = 1
DEC_SEQ = 64
PAST_LEN = 4096

CHUNK = 64
MIX_WIDTH = D_MODEL
A_WIDTH = MIX_WIDTH // 2
A_HEAD_DIM = 64
A_HEADS = A_WIDTH // A_HEAD_DIM
A_KV_HEADS = A_HEADS // 4
A_GROUP = A_HEADS // A_KV_HEADS
A_KV_WIDTH = A_KV_HEADS * A_HEAD_DIM
WINDOW = 128
WIN_CHUNKS = WINDOW // CHUNK
ROT_DIM = A_HEAD_DIM // 4
ROPE_THETA = 500000.0
M_WIDTH = MIX_WIDTH - A_WIDTH
M_HEADS = 4
M_HEAD_DIM = M_WIDTH // M_HEADS
CONV_WIDTH = 4
N_GROUPS = 4
EXPERTS_PER_GROUP = 8
N_EXPERTS = N_GROUPS * EXPERTS_PER_GROUP
TOP_K_INNER = 2
D_EXPERT = D_MODEL // 2
MOE_BLOCK = 128
EPS = 1e-6
SPLIT_SIZES = (A_WIDTH, A_KV_WIDTH, A_KV_WIDTH, 2 * M_WIDTH, M_WIDTH, M_HEADS, M_HEADS, M_WIDTH)
SPLIT_OFFSETS = tuple(int(o) for o in np.cumsum(SPLIT_SIZES)[:-1])
D_IN = sum(SPLIT_SIZES)

kernel_name = 'stream_hybrid_swa_sink_mlstm_hmoe_step'

def rmsnorm(x, g):
    xf = x.astype(jnp.float32)
    y = xf * lax.rsqrt(jnp.mean(xf * xf, axis=-1, keepdims=True) + EPS)
    return (y * g.astype(jnp.float32)).astype(x.dtype)

def modulation(c, w_ada, b_ada):
    mod = (jax.nn.silu(c) @ w_ada + b_ada)[:, None, :]
    return jnp.split(mod, 6, axis=-1)

def ada_norm(x, g, shift, scale):
    return rmsnorm(x, g) * (1 + scale) + shift

def rope_partial(x, pos):
    inv_freq = ROPE_THETA ** (-jnp.arange(0, ROT_DIM, 2, dtype=jnp.float32) / ROT_DIM)
    ang = pos.astype(jnp.float32)[:, None] * inv_freq[None, :]
    cos = jnp.cos(ang)[None, :, None, :]
    sin = jnp.sin(ang)[None, :, None, :]
    xr = x[..., :ROT_DIM].astype(jnp.float32)
    x1, x2 = xr[..., :ROT_DIM // 2], xr[..., ROT_DIM // 2:]
    rot = jnp.concatenate([x1 * cos - x2 * sin, x2 * cos + x1 * sin], axis=-1)
    return jnp.concatenate([rot.astype(x.dtype), x[..., ROT_DIM:]], axis=-1)

def project(h, w_in, pos):
    b, L, _ = h.shape
    q, k, v, qk_m, v_m, ig, fg, o_m = jnp.split(h @ w_in, SPLIT_OFFSETS, axis=-1)
    q = rope_partial(q.reshape(b, L, A_HEADS, A_HEAD_DIM), pos).reshape(b, L, A_KV_HEADS, A_GROUP, A_HEAD_DIM)
    k = rope_partial(k.reshape(b, L, A_KV_HEADS, A_HEAD_DIM), pos)
    v = v.reshape(b, L, A_KV_HEADS, A_HEAD_DIM)
    return q, k, v, qk_m, v_m, ig, fg, o_m

def sink_attend(q, k, v, sinks, mask):
    s = jnp.einsum('...qhgd,...khd->...hgqk', q, k).astype(jnp.float32) * (A_HEAD_DIM ** -0.5)
    if mask is not None:
        s = jnp.where(mask, s, -jnp.inf)
    snk = sinks.astype(jnp.float32).reshape(A_KV_HEADS, A_GROUP, 1, 1)
    mx = jnp.maximum(jnp.max(s, axis=-1, keepdims=True), snk)
    p = jnp.exp(s - mx)
    p = p / (jnp.sum(p, axis=-1, keepdims=True) + jnp.exp(snk - mx))
    return jnp.einsum('...hgqk,...khd->...qhgd', p.astype(v.dtype), v)

def band_attention(q, k, v, sinks):
    b, s_len = q.shape[:2]
    n = s_len // CHUNK
    nk = (WIN_CHUNKS + 1) * CHUNK

    def bands(a):
        ap = jnp.pad(a, ((0, 0), (WIN_CHUNKS * CHUNK, 0), (0, 0), (0, 0)))
        ap = ap.reshape(b, n + WIN_CHUNKS, CHUNK, A_KV_HEADS, A_HEAD_DIM)
        return jnp.concatenate([ap[:, j:j + n] for j in range(WIN_CHUNKS + 1)], axis=2)

    qb = q.reshape(b, n, CHUNK, A_KV_HEADS, A_GROUP, A_HEAD_DIM)
    key_pos = jnp.arange(n)[:, None] * CHUNK + jnp.arange(nk)[None, :] - WIN_CHUNKS * CHUNK
    mask = (key_pos >= 0)[None, :, None, None, None, :]
    out = sink_attend(qb, bands(k), bands(v), sinks, mask)
    return out.reshape(b, s_len, A_WIDTH)

def causal_conv(x, past, w, bias):
    L = x.shape[1]
    xp = jnp.concatenate([past.astype(x.dtype), x], axis=1)
    y = bias + xp[:, 0:L] * w[0]
    for j in range(1, CONV_WIDTH):
        y = y + xp[:, j:j + L] * w[j]
    return y, xp[:, -(CONV_WIDTH - 1):]

def mlstm_prepare(qk_conv, v_m, ig, fg, b_ig, b_fg):
    b, L = v_m.shape[:2]
    q, k = jnp.split(jax.nn.silu(qk_conv).astype(jnp.float32), 2, axis=-1)
    q = q.reshape(b, L, M_HEADS, M_HEAD_DIM) * (M_HEAD_DIM ** -0.5)
    k = k.reshape(b, L, M_HEADS, M_HEAD_DIM)
    v = v_m.astype(jnp.float32).reshape(b, L, M_HEADS, M_HEAD_DIM)
    i_log = ig.astype(jnp.float32) + b_ig.astype(jnp.float32)
    f_log = jax.nn.log_sigmoid(fg.astype(jnp.float32) + b_fg.astype(jnp.float32))
    return q, k, v, i_log, f_log

def mlstm_chunk(C, n, m, q, k, v, i_log, f_log):
    L = q.shape[1]
    bcum = jnp.cumsum(f_log, axis=1).swapaxes(1, 2)
    it = i_log.swapaxes(1, 2)
    causal = jnp.tril(jnp.ones((L, L), dtype=bool))
    dmat = jnp.where(causal, bcum[..., :, None] - bcum[..., None, :] + it[..., None, :], -jnp.inf)
    inter = bcum + m[..., None]
    m_t = jnp.maximum(inter, jnp.max(dmat, axis=-1))
    w_intra = jnp.exp(dmat - m_t[..., None])
    w_inter = jnp.exp(inter - m_t)
    scores = jnp.einsum('blhd,bshd->bhls', q, k) * w_intra
    num = (jnp.einsum('bhls,bshd->blhd', scores, v)
           + w_inter.swapaxes(1, 2)[..., None] * jnp.einsum('bhvd,blhd->blhv', C, q))
    den = jnp.sum(scores, axis=-1) + w_inter * jnp.einsum('bhd,blhd->bhl', n, q)
    h = num / jnp.maximum(jnp.abs(den), jnp.exp(-m_t)).swapaxes(1, 2)[..., None]
    m_new = m_t[..., -1]
    w_end = jnp.exp(bcum[..., -1:] - bcum + it - m_new[..., None])
    decay = jnp.exp(bcum[..., -1] + m - m_new)
    kw = k * w_end.swapaxes(1, 2)[..., None]
    C_new = decay[..., None, None] * C + jnp.einsum('bshv,bshd->bhvd', v, kw)
    n_new = decay[..., None] * n + jnp.sum(kw, axis=1)
    return h, C_new, n_new, m_new

def mlstm_prompt(q, k, v, i_log, f_log):
    b, s_len = q.shape[:2]
    nc = s_len // CHUNK

    def chunks(a):
        return a.reshape((b, nc, CHUNK) + a.shape[2:]).swapaxes(0, 1)

    init = (jnp.zeros((b, M_HEADS, M_HEAD_DIM, M_HEAD_DIM), jnp.float32),
            jnp.zeros((b, M_HEADS, M_HEAD_DIM), jnp.float32),
            jnp.zeros((b, M_HEADS), jnp.float32))

    def step(carry, xs):
        h, C, nv, m = mlstm_chunk(*carry, *xs)
        return (C, nv, m), h

    (C, nv, m), hs = lax.scan(step, init, (chunks(q), chunks(k), chunks(v), chunks(i_log), chunks(f_log)))
    return hs.swapaxes(0, 1).reshape(b, s_len, M_HEADS, M_HEAD_DIM), C, nv, m

def mlstm_output(h, o_pre, g_mh, dtype):
    b, L = h.shape[:2]
    hn = h * lax.rsqrt(jnp.mean(h * h, axis=-1, keepdims=True) + EPS)
    hn = hn.reshape(b, L, M_WIDTH) * g_mh.astype(jnp.float32)
    return (hn * jax.nn.sigmoid(o_pre.astype(jnp.float32))).astype(dtype)

def hier_moe(h, w_rg, b_rg, w_re, b_re, w_g, w_u, w_d):
    b, L, d = h.shape
    t = h.reshape(b * L, d)
    n_tok = t.shape[0]
    lg = (t @ w_rg).astype(jnp.float32) + b_rg.astype(jnp.float32)
    grp = jnp.argmax(lg, axis=-1)
    p_grp = jnp.take_along_axis(jax.nn.softmax(lg, axis=-1), grp[:, None], axis=-1)
    le = ((t @ w_re).astype(jnp.float32) + b_re.astype(jnp.float32)).reshape(n_tok, N_GROUPS, EXPERTS_PER_GROUP)
    le = jnp.take_along_axis(le, grp[:, None, None], axis=1)[:, 0]
    top_v, top_i = lax.top_k(le, TOP_K_INNER)
    gates = (p_grp * jax.nn.softmax(top_v, axis=-1)).reshape(-1)
    eid = (grp[:, None] * EXPERTS_PER_GROUP + top_i).reshape(-1)
    m_rows = eid.shape[0]
    order = jnp.argsort(eid)
    e_sorted = eid[order]
    counts = jnp.bincount(eid, length=N_EXPERTS)
    padded = (counts + MOE_BLOCK - 1) // MOE_BLOCK * MOE_BLOCK
    pad_end = jnp.cumsum(padded)
    dest = (pad_end - padded)[e_sorted] + jnp.arange(m_rows) - (jnp.cumsum(counts) - counts)[e_sorted]
    n_blocks = -(-m_rows // MOE_BLOCK) + N_EXPERTS
    rows = n_blocks * MOE_BLOCK
    src_tok = order // TOP_K_INNER
    xs = jnp.zeros((rows, d), t.dtype).at[dest].set(t[src_tok])
    blk_e = jnp.minimum(jnp.searchsorted(pad_end, jnp.arange(n_blocks) * MOE_BLOCK, side='right'), N_EXPERTS - 1)

    def expert_block(args):
        xb, e = args
        a = jax.nn.silu(xb @ w_g[e]) * (xb @ w_u[e])
        return a @ w_d[e]

    out = lax.map(expert_block, (xs.reshape(n_blocks, MOE_BLOCK, d), blk_e)).reshape(rows, d)
    out_rows = out[dest] * gates[order][:, None].astype(out.dtype)
    y = jnp.zeros_like(t).at[src_tok].add(out_rows)
    return y.reshape(b, L, d)

def residual_update(x, mods, att, hm, o_m, g_mh, w_out, g_ffn, moe_w):
    mixed = jnp.concatenate([att, mlstm_output(hm, o_m, g_mh, x.dtype)], axis=-1) @ w_out
    x = x + mods[2] * mixed
    return x + mods[5] * hier_moe(ada_norm(x, g_ffn, mods[3], mods[4]), *moe_w)

def setup_inputs(seed: int = 0) -> dict:
    key = jax.random.key(seed)
    ks = iter(jax.random.split(key, 32))

    def nrm(shape, scale):
        return jax.random.normal(next(ks), shape, jnp.float32) * scale

    return {
        'x_prompt': nrm((BATCH, SEQ, D_MODEL), 1.0),
        'x_sample': nrm((DEC_BATCH, DEC_SEQ, D_MODEL), 1.0),
        'c_prompt': nrm((BATCH, D_MODEL), 1.0),
        'c_sample': nrm((DEC_BATCH, D_MODEL), 1.0),
        'cache_win_k': nrm((DEPTH, DEC_BATCH, WINDOW, A_KV_HEADS, A_HEAD_DIM), 1.0),
        'cache_win_v': nrm((DEPTH, DEC_BATCH, WINDOW, A_KV_HEADS, A_HEAD_DIM), 1.0),
        'state_conv': nrm((DEPTH, DEC_BATCH, CONV_WIDTH - 1, 2 * M_WIDTH), 1.0),
        'state_C': nrm((DEPTH, DEC_BATCH, M_HEADS, M_HEAD_DIM, M_HEAD_DIM), 0.05),
        'state_n': nrm((DEPTH, DEC_BATCH, M_HEADS, M_HEAD_DIM), 0.2),
        'state_m': nrm((DEPTH, DEC_BATCH, M_HEADS), 1.0),
        'w_ada': nrm((DEPTH, D_MODEL, 6 * D_MODEL), 0.5 * D_MODEL ** -0.5),
        'b_ada': nrm((DEPTH, 6 * D_MODEL), 0.01),
        'g_norm_mix': 1.0 + nrm((DEPTH, D_MODEL), 0.05),
        'g_norm_ffn': 1.0 + nrm((DEPTH, D_MODEL), 0.05),
        'w_in': nrm((DEPTH, D_MODEL, D_IN), D_MODEL ** -0.5),
        'attn_sinks': nrm((DEPTH, A_HEADS), 1.0),
        'conv_w': nrm((DEPTH, CONV_WIDTH, 2 * M_WIDTH), CONV_WIDTH ** -0.5),
        'conv_b': nrm((DEPTH, 2 * M_WIDTH), 0.01),
        'b_igate': nrm((DEPTH, M_HEADS), 0.1),
        'b_fgate': jnp.linspace(3.0, 6.0, M_HEADS)[None, :] + nrm((DEPTH, M_HEADS), 0.1),
        'g_mhnorm': 1.0 + nrm((DEPTH, M_WIDTH), 0.05),
        'w_out': nrm((DEPTH, MIX_WIDTH, D_MODEL), MIX_WIDTH ** -0.5),
        'w_router_group': nrm((DEPTH, D_MODEL, N_GROUPS), D_MODEL ** -0.5),
        'b_router_group': nrm((DEPTH, N_GROUPS), 0.01),
        'w_router_expert': nrm((DEPTH, D_MODEL, N_EXPERTS), D_MODEL ** -0.5),
        'b_router_expert': nrm((DEPTH, N_EXPERTS), 0.01),
        'w_exp_gate': nrm((DEPTH, N_EXPERTS, D_MODEL, D_EXPERT), D_MODEL ** -0.5),
        'w_exp_up': nrm((DEPTH, N_EXPERTS, D_MODEL, D_EXPERT), D_MODEL ** -0.5),
        'w_exp_down': nrm((DEPTH, N_EXPERTS, D_EXPERT, D_MODEL), D_EXPERT ** -0.5),
        'g_final': 1.0 + nrm((D_MODEL,), 0.05),
    }

def reference(x_prompt, x_sample, c_prompt, c_sample, cache_win_k, cache_win_v, state_conv, state_C, state_n, state_m,
              w_ada, b_ada, g_norm_mix, g_norm_ffn, w_in, attn_sinks, conv_w, conv_b, b_igate, b_fgate, g_mhnorm, w_out,
              w_router_group, b_router_group, w_router_expert, b_router_expert, w_exp_gate, w_exp_up, w_exp_down, g_final):
    bp, sp = x_prompt.shape[:2]
    bs, ls = x_sample.shape[:2]
    pos_p = jnp.arange(sp)
    pos_s = PAST_LEN + jnp.arange(ls)
    xp, xs = x_prompt, x_sample
    new_p, new_s = [], []
    for l in range(DEPTH):
        moe_w = (w_router_group[l], b_router_group[l], w_router_expert[l], b_router_expert[l],
                 w_exp_gate[l], w_exp_up[l], w_exp_down[l])
        mods = modulation(c_prompt, w_ada[l], b_ada[l])
        q, k, v, qk_m, v_m, ig, fg, o_m = project(ada_norm(xp, g_norm_mix[l], mods[0], mods[1]), w_in[l], pos_p)
        att = band_attention(q, k, v, attn_sinks[l])
        qk_c, conv_new = causal_conv(qk_m, jnp.zeros((bp, CONV_WIDTH - 1, 2 * M_WIDTH), qk_m.dtype), conv_w[l], conv_b[l])
        hm, C_new, n_new, m_new = mlstm_prompt(*mlstm_prepare(qk_c, v_m, ig, fg, b_igate[l], b_fgate[l]))
        xp = residual_update(xp, mods, att, hm, o_m, g_mhnorm[l], w_out[l], g_norm_ffn[l], moe_w)
        new_p.append((k[:, -WINDOW:], v[:, -WINDOW:], conv_new, C_new, n_new, m_new))
        mods = modulation(c_sample, w_ada[l], b_ada[l])
        q, k, v, qk_m, v_m, ig, fg, o_m = project(ada_norm(xs, g_norm_mix[l], mods[0], mods[1]), w_in[l], pos_s)
        k_all = jnp.concatenate([cache_win_k[l].astype(k.dtype), k], axis=1)
        v_all = jnp.concatenate([cache_win_v[l].astype(v.dtype), v], axis=1)
        att = sink_attend(q, k_all, v_all, attn_sinks[l], None).reshape(bs, ls, A_WIDTH)
        qk_c, conv_new = causal_conv(qk_m, state_conv[l], conv_w[l], conv_b[l])
        hm, C_new, n_new, m_new = mlstm_chunk(state_C[l].astype(jnp.float32), state_n[l].astype(jnp.float32),
                                              state_m[l].astype(jnp.float32),
                                              *mlstm_prepare(qk_c, v_m, ig, fg, b_igate[l], b_fgate[l]))
        xs = residual_update(xs, mods, att, hm, o_m, g_mhnorm[l], w_out[l], g_norm_ffn[l], moe_w)
        new_s.append((k_all[:, -WINDOW:], v_all[:, -WINDOW:], conv_new, C_new, n_new, m_new))
    win_k_p, win_v_p, conv_p, C_p, n_p, m_p = [jnp.stack(a) for a in zip(*new_p)]
    win_k_s, win_v_s, conv_s, C_s, n_s, m_s = [jnp.stack(a) for a in zip(*new_s)]
    y_prompt = rmsnorm(xp, g_final)
    y_sample = rmsnorm(xs, g_final)
    return (y_prompt, y_sample, win_k_p, win_v_p, conv_p, C_p, n_p, m_p, win_k_s, win_v_s, conv_s, C_s, n_s, m_s)


_drawn_inputs = setup_inputs


def setup_inputs(seed=0):
    import zlib

    import numpy as np

    out = dict(_drawn_inputs(seed))
    spreads = {}
    factors = {'state_C': 8.0,
     'state_n': 8.0,
     'state_m': 8.0,
     'g_norm_ffn': 2.987,
     'attn_sinks': 8.0,
     'conv_b': 3.488,
     'g_mhnorm': 6.783,
     'b_router_group': 8.0,
     'b_router_expert': 8.0}
    for name, (base, spread) in spreads.items():
        noise = np.random.default_rng([zlib.crc32(name.encode()), seed]).standard_normal(out[name].shape)
        drawn = base * np.exp(spread * noise) if base else spread * noise
        out[name] = jnp.asarray(drawn.astype(out[name].dtype))
    for name, factor in factors.items():
        out[name] = (out[name] * factor).astype(out[name].dtype)
    return out
```

```python
from contextlib import ExitStack

import concourse.bass as bass
from concourse import mybir

F32 = mybir.dt.float32
I32 = mybir.dt.int32
U32 = mybir.dt.uint32
ALU = mybir.AluOpType
ACT = mybir.ActivationFunctionType
AX = mybir.AxisListType

P = 128
D = 1024
KT = D // P
SEQ, DEC, PAST = 2048, 64, 4096
NPT = SEQ // P
NT = NPT + 1
SAMPLE = NT - 1
CHUNK = 64
HD = 64
NH, NKV = 8, 2
G = NH // NKV
ROT = HD // 4
MH, MD = 4, 128
CW = 4
NG, EPG = 4, 8
NE = NG * EPG
FE = D // 2
FT = FE // P
CAP = NT
NB = NE * CAP
SLOTS = NB * P
TRASH = 2 * NT * P
EPS = 1e-6
BIG = 1e30
Q0, K0, C0, VM0, I0, F0, O0, DIN = 0, 512, 768, 1792, 2304, 2336, 2340, 2852
NADA = 6 * D // 512

STEPS = {"dve": 88, "act": 18, "pool": 6}


class Steps:

    def __init__(self, eng, s):
        self.eng, self.s, self.base, self.n = eng, s, 0, 0

    def __call__(self, ins):
        self.n += 1
        ins.then_inc(self.s, 1)
        self.eng.wait_ge(self.s, self.base + self.n)


def has(t):
    return not isinstance(t, int) or 0 <= t < NT


def walk(eng, turn, steps=None, per_turn=0):
    turn(0, 0)
    turn(1, 1)
    pairs = NPT // 2 - 2
    start = steps.n if steps else 0
    with eng.Fori(0, pairs) as i:
        if steps:
            steps.base, steps.n = i * per_turn, start
        turn(2 * i + 2, 0)
        turn(2 * i + 3, 1)
    if steps:
        if steps.n - start != per_turn:
            raise ValueError(f"{steps.s}: {steps.n - start} steps in a pair of turns, not {per_turn}")
        steps.base, steps.n = 0, start + pairs * per_turn
    turn(NPT - 2, 0)
    turn(NPT - 1, 1)
    turn(NPT, 0)
    turn(NT, 1)
    turn(NT + 1, 0)


def past(v):
    return not isinstance(v, int) or v > 0


def upto(v):
    return min(v, NT) if isinstance(v, int) else v


def build(nc, a, o):
    with ExitStack() as ctx:
        def sb(name, shape, dt=F32):
            return ctx.enter_context(nc.sbuf_tensor(name, shape, dt))

        def dram(name, shape):
            return nc.dram_tensor(name, shape, F32, kind="Internal").ap()

        S = {}

        def sem(name):
            if name not in S:
                S[name] = ctx.enter_context(nc.semaphore(name))
            return S[name]

        def apart(eng):
            eng.sem_inc(sem("apart"), 1)

        mods_d = dram("mods_d", [2, 6 * D])
        x1_d = dram("x1_d", [NT * P, D])
        h2_d = dram("h2_d", [NT * P, D])
        list_d = dram("list_d", [SLOTS + 2 * P, 1])
        rows_d = dram("rows_d", [TRASH + P, D])

        big = sb("big", [P, KT * DIN + KT * D])
        w_in = big[:, 0:KT * DIN].rearrange("p (k n) -> p k n", k=KT)
        w_out = big[:, KT * DIN:KT * DIN + KT * D].rearrange("p (k n) -> p k n", k=KT)
        ada = [big[:, KT * DIN + i * KT * 512:KT * DIN + (i + 1) * KT * 512].rearrange("p (k n) -> p k n", k=KT)
               for i in range(2)]
        WE = KT * FE
        ident = sb("ident", [P, P])
        cmask = sb("cmask", [P, P])
        lower = sb("lower", [P, P])
        ones = sb("ones", [P, P])
        negones = sb("negones", [MH, P])
        amask = sb("amask", [P, 3, 2 * P])
        iotas = sb("iotas", [P, NG + 2 * NE])
        tokid = sb("tokid", [P, NT])
        padcol = sb("padcol", [P, 3])
        eps_c = sb("eps_c", [P, 1])
        one_c = sb("one_c", [P, 1])
        w_r = sb("w_r", [P, KT, NG + NE])
        b_r = sb("b_r", [P, NG + NE])
        taps = sb("taps", [P, CW + 1, KT])
        g_mh = sb("g_mh", [P, MH, MD])
        sinks = sb("sinks", [P, NH])
        b_i = sb("b_i", [MH, 1])
        b_f = sb("b_f", [MH, 1])
        mixc = sb("mixc", [P, 2, 2, KT])
        cc = sb("cc", [P, KT, 2])
        cs = sb("cs", [P, KT, 2])
        row_gate = sb("row_gate", [P, D])
        row_g2 = sb("row_g2", [P, D])
        row_s2 = sb("row_s2", [P, D])
        xr = sb("xr", [P, D])
        rope_t = sb("rope_t", [P, 2 * ROT])
        hT = sb("hT", [P, KT, P])
        qkv = sb("qkv", [P, 12, HD])
        vmo = sb("vmo", [P, MH, MD + 1])
        og = sb("og", [P, MH, MD])
        cT = sb("cT", [P, KT, CW - 1 + P])
        hist = [sb("hist_p", [P, CW - 1, KT]), sb("hist_s", [P, CW - 1, KT])]
        hist_in = sb("hist_in", [P, CW - 1, KT])
        y = sb("y", [P, KT, P])
        sm = sb("sm", [P, 4, 2 * P])
        smf = sm[:, :, :].rearrange("p a b -> p (a b)")
        yf = y[:, :, :].rearrange("p a b -> p (a b)")
        rt = sb("rt", [P, 2, 10, ROT])
        qT = sb("qT", [P, G, P])
        kT = [sb("kT0", [P, P]), sb("kT1", [P, P])]
        kTs = sb("kTs", [P, P])
        vk = [sb("vk0", [P, NKV, HD]), sb("vk1", [P, NKV, HD])]
        vs = sb("vs", [P, NKV, HD])
        pT = sb("pT", [P, 2, 4, P])
        pTf = pT[:, :, :, :].rearrange("p a b c -> p (a b c)")
        wT = sb("wT", [P, MH, P])
        kw = sb("kw", [P, MH, MD])
        C_p = sb("C_pr", [P, MH, MD + 1])
        C_s = sb("C_sa", [P, MH, MD + 1])
        mix = sb("mix", [P, D])
        mT = sb("mT", [P, KT, P])
        num = sb("num", [P, MH, MD + 1])
        md = num[0:MH, :, 0:P]
        gr = sb("gr", [MH, 6, P])
        stk = sb("stk", [P, P])
        cols = sb("cols", [P, P])
        dec = sb("dec", [P, MH])
        dd = sb("dd", [MH, MH])
        m_st = [sb("m_st0", [MH, 1]), sb("m_st1", [MH, 1])]
        m_sa = sb("m_sa", [MH, 1])
        g1c = sb("g1c", [MH, 2])
        at4 = sb("at4", [P, 8, 4])
        ml4 = sb("ml4", [P, 8, 4])
        nr = sb("nr", [P, 8])
        lg8 = sb("lg8", [P, 8])
        le = sb("le", [P, NE])
        gm8 = sb("gm8", [P, 8])
        gi8 = sb("gi8", [P, 8], U32)
        lv8 = sb("lv8", [P, 8])
        li8 = sb("li8", [P, 8], U32)
        rc = sb("rc", [P, 16])
        gmk = sb("gmk", [P, 2, NG])
        oh = sb("oh", [P, 5, NE])
        Msum = sb("Msum", [P, NE])
        dst = sb("dst", [P, 2], I32)
        gate_all = sb("gate_all", [P, 2, NT])
        tok_s = sb("tok_s", [P, 2])
        sidx_f = sb("sidx_f", [P, 1])
        sidx = sb("sidx", [P, 1], I32)
        cnt_f = sb("cnt_f", [1, 4, NE])
        cnt_i = sb("cnt_i", [1, 3, NE], I32)
        idx_all = yf[:, 0:NB].bitcast(I32)
        sidx_all = mT[:, :, :].rearrange("p a b -> p (a b)")[:, 0:NB].bitcast(I32)
        idx = sb("idx", [P, 1], I32)
        num_f = pT[:, :, :, :].rearrange("p a b c -> p (a b c)")[:, 0:NB]
        lists = smf[:, 0:5 * P].rearrange("p (a b) -> p a b", a=5)
        xg, xT, aT, eT, yrow = xr, hT, qT, wT, mix
        pieces = [big[:, j * D:(j + 1) * D] for j in range(30)]
        pieces += [smf, cT[:, :, :].rearrange("p a b -> p (a b)")[:, 0:D], pTf, row_gate[:], row_g2[:], row_s2[:]]
        WE_IN = (48, 48, 16 * (1 + 3 + 4))
        NW = WE // D
        we = [[pieces[(3 * i + j) * NW:(3 * i + j + 1) * NW] for j in range(3)] for i in range(3)]
        f_r = [[big[:, (4 * i + j) * D:(4 * i + j + 1) * D] for j in range(4)] for i in range(2)]
        f_g = [sb("f_g0", [P, 2]), sb("f_g1", [P, 2])]

        b0 = ctx.enter_context(nc.psum_tensor("b0", [P, 512], F32))
        b1 = ctx.enter_context(nc.psum_tensor("b1", [P, 512], F32))
        b2 = ctx.enter_context(nc.psum_tensor("b2", [P, 512], F32))
        b34 = ctx.enter_context(nc.psum_tensor("b34", [P, 1024], F32))
        b56 = ctx.enter_context(nc.psum_tensor("b56", [P, 1024], F32))
        b7 = ctx.enter_context(nc.psum_tensor("b7", [P, 512], F32))

        def row(ap):
            return ap.rearrange("(a n) -> a n", a=1)

        def rows(t):
            return slice(t * P, t * P + P) if isinstance(t, int) else bass.ds(t * P, P)

        def one(t):
            return slice(t, t + 1) if isinstance(t, int) else bass.ds(t, 1)

        def prev(t, p, own, sample):
            return sample if isinstance(t, int) and t in (0, SAMPLE) else own[1 - p]

        def head2(bank, h):
            at = (h // 2) * 512 + (h % 2) * (MD + 1)
            return bank[:, at:at + MD + 1]

        ctx.enter_context(nc.allow_non_contiguous_dma(reason="a few small columns"))
        block = ctx.enter_context(nc.Block())

        @block.sync
        def _(sp):
            def move(name, to, frm):
                sp.dma_start(to, frm).then_inc(sem(name), 16)

            for j in range(0, NB + 2, P):
                n = min(P, NB + 2 - j)
                move("list_init", list_d[j * P:(j + n) * P, :].rearrange("(b s) a -> b (s a)", s=P), a["c_trash"][0:n, :])
            move("c_in", cc[:], a["c_both"].rearrange("(p k) s -> p k s", k=KT))
            for i in range(NADA):
                if past(i - 1):
                    sp.wait_ge(sem("ada_mm"), i - 1)
                move(f"ada_in{i % 2}", ada[i % 2],
                     a["w_ada"].rearrange("(p k) n -> p k n", k=KT)[:, :, i * 512:i * 512 + 512])
                if i == 0:
                    for s_ in range(2):
                        move("small_in", mT[s_:s_ + 1, :, :].rearrange("p a b -> p (a b)"), row(a["g_mix"]))
                        move("small_in", hT[s_:s_ + 1, :, :].rearrange("p a b -> p (a b)"), row(a["g_ffn"]))
                    for j in range(NADA):
                        buf = (y, sm, xr, mix, row_gate, row_g2)[j // 2]
                        bb = buf[0:2, (j % 2) * 512:(j % 2) * 512 + 512] if buf in (xr, mix, row_gate, row_g2) else \
                            (yf if buf is y else smf)[0:2, (j % 2) * 512:(j % 2) * 512 + 512]
                        move("small_in", bb, row(a["b_ada"][j * 512:j * 512 + 512]).broadcast_to([2, 512]))
                if i == 1:
                    for to, name in ((ident[:], "c_ident"), (cmask[:], "c_cmask"), (lower[:], "c_lower"),
                                     (amask[:], "c_amask"), (iotas[:], "c_iotas"), (tokid[:], "c_tokid"),
                                     (padcol[:], "c_padcol"), (taps[:], "taps")):
                        move("const_in", to, a[name])
                    move("const_in", sidx_f[:], a["c_trash"][0, :].rearrange("(n a) -> n a", a=1))
                    move("const_in", w_r[:], a["w_r"].rearrange("(p k) n -> p k n", k=KT))
                    move("const_in", b_r[:], row(a["b_r"]).broadcast_to([P, NG + NE]))
                    move("const_in", g_mh[:, :, :].rearrange("p a b -> p (a b)"), row(a["g_mh"]).broadcast_to([P, MH * MD]))
                    move("const_in", sinks[:], row(a["sinks"]).broadcast_to([P, NH]))
                    move("const_in", b_i[:], a["b_ig"].rearrange("(n a) -> n a", a=1))
                    move("const_in", b_f[:], a["b_fg"].rearrange("(n a) -> n a", a=1))
                    move("const_in", kw[:], a["state_C"].rearrange("h v k -> v h k"))
                    move("const_in", C_s[:, :, MD], a["state_n"].rearrange("h k -> k h"))
                    move("const_in", m_sa[:], a["state_m"].rearrange("(n a) -> n a", a=1))
                    move("const_in", qT[:, 0, :], a["cache_k"])
                    move("const_in", vs[:].rearrange("p a b -> p (a b)"), a["cache_v"])
                    move("const_in", hist_in[:], a["state_conv"])
                if i == 4:
                    for k in range(KT):
                        move("win_in", w_in[:, k, :], a["w_in"].rearrange("(p k) n -> p k n", k=KT)[:, k, :])
            sp.wait_ge(sem("ada_mm"), NADA)
            move("wout_in", w_out, a["w_out"].rearrange("(p k) n -> p k n", k=KT))
            for i in range(NADA):
                sp.wait_ge(sem("ada_row"), i + 1)
                buf = (yf, smf, xr, mix, row_gate, row_g2)[i // 2]
                move("mods_out", mods_d[:, i * 512:i * 512 + 512], buf[0:2, (i % 2) * 512:(i % 2) * 512 + 512])
            sp.wait_ge(sem("mods_out"), 16 * NADA)
            move("x_in", smf, a["x"][0:P, :])
            for s_ in range(2):
                for j, m in enumerate((1, 0)):
                    move("modc_in", mixc[:, s_, j, :],
                         mods_d[s_, m * D:(m + 1) * D].rearrange("(p k) -> p k", k=KT))

            def modrow(to, s_, m, name="rows_in"):
                move(name, to[:], mods_d[s_:s_ + 1, m * D:(m + 1) * D].broadcast_to([P, D]))

            modrow(row_gate, 0, 2)
            modrow(row_s2, 0, 3)
            modrow(row_g2, 0, 4)

            def load_x(t, p):
                if isinstance(t, int) and t == 0:
                    return
                if past(t):
                    sp.wait_ge(sem("g_n1"), t)
                if past(t - 1):
                    sp.wait_ge(sem("g_pt1"), t - 1)
                move("x_in", smf, a["x"][rows(t), :])

            def load_rope(t, p):
                if past(t):
                    sp.wait_ge(sem("rope_ok"), t)
                move("rope_in", rope_t[:], a["rope"][rows(t), :])

            def load_xr(t, p):
                if past(32 * t):
                    sp.wait_ge(sem("st_done"), 32 * t)
                move("xr_in", xr[:], a["x"][rows(t), :])

            def windows(t, p):
                if isinstance(t, int) and t in (NPT - 1, SAMPLE):
                    s_, n = ("p", P) if t < NPT else ("s", DEC)
                    sp.wait_ge(sem("rope_ok"), t + 1)
                    sp.wait_ge(sem("c_kv"), t + 1)
                    move("kv_out", o[f"k_{s_}"][P - n:P, :], qkv[0:n, 8:10, :].rearrange("p a b -> p (a b)"))
                    move("kv_out", o[f"v_{s_}"][P - n:P, :], qkv[0:n, 10:12, :].rearrange("p a b -> p (a b)"))
                    if t == SAMPLE:
                        move("win_out", o["k_s"][0:P - n, :], a["cache_k"][n:P, :])
                        move("win_out", o["v_s"][0:P - n, :], a["cache_v"][n:P, :])
                    sp.wait_ge(sem("conv_ok"), t + 1)
                    move("win_out", o[f"conv_{s_}"], hist[t == SAMPLE][:])

            def states(t, p):
                if isinstance(t, int) and t in (NPT - 1, SAMPLE):
                    s_ = "p" if t < NPT else "s"
                    sp.wait_ge(sem("state_ok"), 1 + (t == SAMPLE))
                    move("state_out", o[f"C_{s_}"].rearrange("h v k -> v h k"), kw[:])
                    move("state_out", o[f"n_{s_}"].rearrange("h k -> k h"), (C_p, C_s)[t == SAMPLE][:, :, MD])
                    move("state_out", o[f"m_{s_}"].rearrange("(n a) -> n a", a=1), m_st[p][:])

            def stores(t, p):
                sp.wait_ge(sem("h2"), t + 1)
                move("st_done", x1_d[rows(t), :], xr[:])
                move("st_done", h2_d[rows(t), :], mix[:])
                if isinstance(t, int) and t == NPT - 1:
                    modrow(row_gate, 1, 2)
                    modrow(row_s2, 1, 3)
                    modrow(row_g2, 1, 4)

            def turn(t, p):
                if has(t - 1):
                    load_xr(t - 1, 1 - p)
                    windows(t - 1, 1 - p)
                if has(t):
                    load_rope(t, p)
                if has(t - 1):
                    states(t - 1, 1 - p)
                if has(t + 1):
                    load_x(t + 1, 1 - p)
                if has(t - 1):
                    stores(t - 1, 1 - p)

            load_x(0, 0)
            walk(sp, turn)

            def weights(e, k, which=(0, 1, 2)):
                for j in which:
                    name = ("w_g", "w_u", "w_d")[j]
                    src = a[name][e] if isinstance(e, int) else a[name][bass.ds(e, 1), :, :]
                    src = src.rearrange("(p k) n -> p (k n)" if isinstance(e, int) else "a (p k) n -> p (a k n)", p=P)
                    at = 0
                    while at < NW:
                        n = 1
                        first = (3 * k + j) * NW + at
                        while at + n < NW and first + n < 30:
                            n += 1
                        to = big[:, first * D:(first + n) * D] if first < 30 else pieces[first]
                        move(f"we_in{k}", to, src[:, at * D:(at + n) * D])
                        at += n

            sp.wait_ge(sem("g_o"), NT)
            weights(0, 0)
            weights(1, 1, (0, 1))
            sp.wait_ge(sem("scat"), 32 * NT)
            sp.wait_ge(sem("h2"), NT)
            sp.wait_ge(sem("g_hT1"), NT)
            for j in range(5):
                n = min(P, NB - j * P)
                move("lists_in", lists[0:n, j, :], list_d[j * P * P:(j * P + n) * P, :].rearrange("(b s) a -> b (s a)", s=P))
            sp.wait_ge(sem("g_pr1"), NT)
            weights(1, 1, (2,))
            sp.wait_ge(sem("idx_ok"), 1)
            weights(2, 2)
            sp.wait_ge(sem("cnt_ok"), 1)

            def used(e):
                return sp.value_load(cnt_i[0:1, 1, bass.ds(e + 1, 1)], min_val=0, max_val=NB)

            with sp.Fori(0, NE // 3 - 1) as i:
                for k in range(3):
                    sp.wait_ge(sem("dn"), used(3 * i + k))
                    weights(3 * i + k + 3, k)
            for k in range(3):
                sp.wait_ge(sem("dn"), used(NE // 3 * 3 - 3 + k))
                if k < NE % 3:
                    weights(NE // 3 * 3 + k, k)
            modrow(row_gate, 0, 5, "rows4_in")
            modrow(row_s2, 1, 5, "rows4_in")
            move("rows4_in", row_g2[:], row(a["g_final"]).broadcast_to([P, D]))

            blocks = sp.value_load(cnt_i[0:1, 2, 0:1], min_val=0, max_val=NB)
            sp.wait_ge(sem("dn"), blocks)
            sp.wait_ge(sem("row_st"), 16 * blocks + 16)

            def out_tile(t, k, half):
                n = DEC if isinstance(t, int) and t == SAMPLE else P
                if not (isinstance(t, int) and t < 2):
                    sp.wait_ge(sem("f_x"), t - 1)
                    sp.wait_ge(sem(f"y_out{k}"), 16 * half)
                r = slice(t * P, t * P + n) if isinstance(t, int) else bass.ds(t * P, P)
                r1 = slice(NT * P + t * P, NT * P + t * P + n) if isinstance(t, int) else bass.ds(NT * P + t * P, P)
                move(f"x1_in{k}", f_r[k][0][0:n, :], rows_d[r, :])
                move(f"x1_in{k}", f_r[k][1][0:n, :], rows_d[r1, :])
                move(f"x1_in{k}", f_r[k][2][0:n, :], x1_d[r, :])

            def y_store(t, k, half):
                sp.wait_ge(sem("y_ok"), t + 1)
                if isinstance(t, int) and t == SAMPLE:
                    move(f"y_out{k}", o["y_s"], f_r[k][3][0:DEC, :])
                else:
                    move(f"y_out{k}", o["y_p"][rows(t), :], f_r[k][3][:])

            out_tile(0, 0, 0)
            out_tile(1, 1, 0)
            with sp.Fori(0, NPT // 2 - 1) as i:
                y_store(2 * i, 0, i)
                out_tile(2 * i + 2, 0, i + 1)
                y_store(2 * i + 1, 1, i)
                out_tile(2 * i + 3, 1, i + 1)
            y_store(NPT - 2, 0, 0)
            out_tile(SAMPLE, 0, NPT // 2)
            y_store(NPT - 1, 1, 0)
            y_store(SAMPLE, 0, 0)
            sp.wait_ge(sem("y_out0"), 16 * (NPT // 2 + 1))
            sp.wait_ge(sem("y_out1"), 16 * (NPT // 2))
            sp.wait_ge(sem("kv_out"), 16 * 4)
            sp.wait_ge(sem("win_out"), 16 * 4)
            sp.wait_ge(sem("state_out"), 16 * 6)
            sp.wait_ge(sem("st_done"), 32 * NT)

        @block.gpsimd
        def _(pool):
            st = Steps(pool, sem("pool_step"))

            def rotate(t, p):
                pool.wait_ge(sem("rope_in"), 16 * (t + 1))
                pool.wait_ge(sem("c_q"), t + 1)
                pool.wait_ge(sem("c_kv"), t + 1)
                qk = qkv[:, 0:10, :]
                cos = rope_t[:, 0:ROT].rearrange("p (a c) -> p a c", a=1).broadcast_to([P, 10, ROT])
                msin = rope_t[:, ROT:ROT + 8].rearrange("p (a c) -> p a c", a=1).broadcast_to([P, 10, 8])
                sin = rope_t[:, ROT + 8:2 * ROT].rearrange("p (a c) -> p a c", a=1).broadcast_to([P, 10, 8])
                pool.tensor_tensor(rt[:, 0, :, :], qk[:, :, 0:ROT], cos, ALU.mult)
                pool.tensor_tensor(rt[:, 1, :, 0:8], qk[:, :, 8:16], msin, ALU.mult)
                st(pool.tensor_tensor(rt[:, 1, :, 8:16], qk[:, :, 0:8], sin, ALU.mult))
                pool.tensor_tensor(qk[:, :, 0:ROT], rt[:, 0, :, :], rt[:, 1, :, :], ALU.add).then_inc(sem("rope_ok"), 1)
                if past(t):
                    pool.wait_ge(sem("g_pv1"), t)
                apart(pool)
                pool.tensor_copy(vk[p][:], qkv[:, 10:12, :]).then_inc(sem("vk_ok"), 1)

            def scatter(t, p):
                if past(32 * t):
                    pool.wait_ge(sem("scat"), 32 * t)
                apart(pool)
                pool.wait_ge(sem("dst_ok"), t + 1)
                st(pool.tensor_copy(tok_s[:, 0:1], tokid[:, one(t)]))
                apart(pool)
                st(pool.tensor_scalar(tok_s[:, 1:2], tok_s[:, 0:1], float(NT * P), 0.0, ALU.add, ALU.add))
                apart(pool)
                for k in range(2):
                    pool.indirect_dma_start(list_d, bass.IndirectOffsetOnAxis(ap=dst[:, k:k + 1], axis=0),
                                            tok_s[:, k:k + 1], None).then_inc(sem("scat"), 16)

            pool.wait_ge(sem("list_init"), 16 * 5)
            pool.wait_ge(sem("const_in"), 16 * 21)
            def turn(t, p):
                if has(t - 2):
                    scatter(t - 2, p)
                if has(t):
                    rotate(t, p)

            walk(pool, turn, st, STEPS["pool"])

            st(pool.tensor_copy(sidx[:], sidx_f[:]))
            pool.wait_ge(sem("idx_ok"), 1)
            pool.wait_ge(sem("cnt_ok"), 1)
            pool.wait_ge(sem("st_done"), 32 * NT)
            with pool.Fori(0, NE) as e:
                n = pool.value_load(cnt_i[0:1, 0, bass.ds(e, 1)], min_val=1, max_val=CAP)
                g0 = pool.value_load(cnt_i[0:1, 1, bass.ds(e, 1)], min_val=0, max_val=NB)
                with pool.Fori(0, n) as b:
                    pool.wait_ge(sem("g_x1"), g0 + b + 1)
                    apart(pool)
                    pool.tensor_copy(idx[:], idx_all[:, bass.ds(e * CAP + b, 1)]).then_inc(sem("idx1"), 1)
                    pool.wait_ge(sem("idx1"), g0 + b + 1)
                    apart(pool)
                    pool.indirect_dma_start(xg[:], None, h2_d, bass.IndirectOffsetOnAxis(ap=idx[:], axis=0)).then_inc(sem("gath"), 16)
                    pool.wait_ge(sem("ye"), g0 + b + 1)
                    apart(pool)
                    pool.indirect_dma_start(rows_d, bass.IndirectOffsetOnAxis(ap=sidx[:], axis=0), yrow[:], None).then_inc(sem("row_st"), 16)
                    pool.wait_ge(sem("row_st"), 16 * (g0 + b + 1))
                    apart(pool)
                    pool.tensor_copy(sidx[:], sidx_all[:, bass.ds(e * CAP + b, 1)]).then_inc(sem("sidx1"), 1)
                    pool.wait_ge(sem("sidx1"), g0 + b + 1)

            blocks = pool.value_load(cnt_i[0:1, 2, 0:1], min_val=0, max_val=NB)
            pool.wait_ge(sem("ye"), blocks + 1)
            apart(pool)
            pool.indirect_dma_start(rows_d, bass.IndirectOffsetOnAxis(ap=sidx[:], axis=0), yrow[:], None).then_inc(sem("row_st"), 16)

        @block.scalar
        def _(act):
            st = Steps(act, sem("act_step"))
            A = nc.scalar.activation
            copy = ACT.Copy

            act.preload_act_table_set("natural_log_exp_and_others")
            act.wait_ge(sem("c_in"), 16)
            A(cs[:], cc[:], ACT.Exp, scale=-1.0).then_inc(sem("c_exp"), 1)

            def norm(t, p):
                act.wait_ge(sem("x_in"), 16 * (t + 1))
                if past(t - 1):
                    act.wait_ge(sem("c_delta"), t - 1)
                if isinstance(t, int) and t - 2 == NPT - 1:
                    act.wait_ge(sem("state_ok"), 1)
                st(A(b56[:], smf, ACT.Square, accum_out=nr[:, 0:1]))
                st(A(nr[:, 1:2], nr[:, 0:1], ACT.Ln, bias=eps_c[:, 0:1], scale=1.0 / D))
                st(A(nr[:, 2:3], nr[:, 1:2], ACT.Exp, scale=-0.5))
                A(smf, smf, copy, scale=nr[:, 2:3]).then_inc(sem("xn_ok"), 1)

            def evac_q(t, p):
                act.wait_ge(sem("g_q"), t + 1)
                if past(t):
                    act.wait_ge(sem("g_tk"), t)
                if past(t):
                    act.wait_ge(sem("vk_ok"), t)
                if isinstance(t, int) and t == SAMPLE:
                    act.wait_ge(sem("kv_out"), 32)
                A(qkv[:, 0:8, :].rearrange("p a b -> p (a b)"), b2[:], copy).then_inc(sem("c_q"), 1)

            def evac_kv(t, p):
                act.wait_ge(sem("g_kv"), t + 1)
                A(qkv[:, 8:12, :].rearrange("p a b -> p (a b)"), b0[:, 0:256], copy).then_inc(sem("c_kv"), 1)

            def evac_c(i, bank):
                def f(t, p):
                    act.wait_ge(sem(f"g_qk{i}"), t + 1)
                    if past(t):
                        act.wait_ge(sem("conv_ok"), t)
                    A(cT[:, 4 * i:4 * i + 4, CW - 1:], bank[:].rearrange("p (a b) -> p a b", a=4), copy)\
                        .then_inc(sem(f"c_qk{i}"), 1)
                return f

            def evac_vm(t, p):
                act.wait_ge(sem("g_vm"), t + 1)
                if past(t):
                    act.wait_ge(sem("g_delta"), t)
                A(vmo[:, :, 0:MD], b1[:].rearrange("p (a b) -> p a b", a=MH), copy).then_inc(sem("c_vm"), 1)

            def evac_o(t, p):
                act.wait_ge(sem("g_o"), t + 1)
                if past(t):
                    act.wait_ge(sem("mixed_h"), t)
                A(og[:].rearrange("p a b -> p (a b)"), b7[:], ACT.Exp, scale=-1.0).then_inc(sem("c_o"), 1)

            def sig_o(t, p):
                act.wait_ge(sem("o_1e"), t + 1)
                st(A(og[:], og[:], ACT.Ln))
                A(og[:], og[:], ACT.Exp, scale=-1.0).then_inc(sem("o_sig"), 1)

            def prep(t, p):
                act.wait_ge(sem("conv_y"), t + 1)
                if past(t):
                    act.wait_ge(sem("g_pv1"), t)
                A(pTf, yf, ACT.Exp, scale=-1.0).then_inc(sem("silu_e"), 1)
                act.wait_ge(sem("silu_1e"), t + 1)
                st(A(pTf, pTf, ACT.Ln))
                A(pTf, pTf, ACT.Exp, scale=-1.0).then_inc(sem("silu_s"), 1)

            def gate(t, p):
                act.wait_ge(sem("f_neg"), t + 1)
                st(A(gr[:, 2, :], gr[:, 2, :], ACT.Exp))
                A(gr[:, 2, :], gr[:, 2, :], ACT.Ln, bias=one_c[0:MH, 0:1]).then_inc(sem("f_log"), 1)
                m_in = m_sa if isinstance(t, int) and t == SAMPLE else m_st[1 - p]
                act.wait_ge(sem("gate_m"), t + 1)
                A(stk[32:32 + MH, :], stk[0:MH, :], ACT.Exp, bias=g1c[:, 0:1])
                A(stk[64:64 + MH, :], gr[:, 4, :], ACT.Exp, bias=m_in[:, 0:1], scale=-1.0)
                A(stk[96:96 + MH, :], gr[:, 5, :], ACT.Exp, scale=-1.0)
                A(g1c[:, 1:2], gr[:, 4, P - 1:P], ACT.Exp, bias=m_in[:, 0:1], scale=-1.0).then_inc(sem("gate_e"), 1)

            def kr(t, p):
                act.wait_ge(sem("g_kr"), t + 1)
                act.wait_ge(sem("c_cols"), t + 1)
                if isinstance(t, int) and t == SAMPLE:
                    act.wait_ge(sem("state_out"), 48)
                for h in range(MH):
                    last = A(kw[:, h, :], b56[:, h * MD:(h + 1) * MD], copy, scale=cols[:, 32 + h:33 + h])
                last.then_inc(sem("c_kw"), 1)

            def probs(j):
                def f(t, p):
                    act.wait_ge(sem(f"smax{j}"), t + 1)
                    for g in range(G):
                        A(sm[:, g, :], sm[:, g, :], ACT.Exp, bias=at4[:, 1, g:g + 1], scale=HD ** -0.5,
                          accum_out=at4[:, 2, g:g + 1])
                    A(at4[:, 3, :], at4[:, 3, :], ACT.Exp).then_inc(sem(f"probs{j}"), 1)
                return f

            def w_exp(t, p):
                act.wait_ge(sem("w_arg"), t + 1)
                for h in range(MH):
                    last = A(wT[:, h, :], wT[:, h, :], ACT.Exp, bias=cols[:, h:h + 1])
                last.then_inc(sem("w_exp"), 1)

            def probs_t(j):
                def f(t, p):
                    act.wait_ge(sem(f"g_pt{j}"), t + 1)
                    A(pT[:, 1, :, :], b34[:, 512:1024].rearrange("p (a b) -> p a b", a=4), copy).then_inc(sem(f"c_pta{j}"), 1)
                return f

            def inter(t, p):
                act.wait_ge(sem("g_inter"), t + 1)
                act.wait_ge(sem("g_negm"), t + 1)
                for h in range(MH):
                    last = A(num[:, h, :], head2(b34, h), copy, scale=cols[:, 64 + h:65 + h])
                last.then_inc(sem("c_inter"), 1)

            def mid(t, p):
                act.wait_ge(sem("c_num"), t + 1)
                act.wait_ge(sem("g_intra"), t + 1)
                for h in range(MH):
                    last = A(wT[:, h, :], num[:, h, 0:MD], ACT.Square, accum_out=ml4[:, 2, h:h + 1])
                last.then_inc(sem("h_sq"), 1)
                act.wait_ge(sem("h_ms"), t + 1)
                st(A(ml4[:, 4, :], ml4[:, 3, :], ACT.Ln, bias=eps_c[:, 0:1], scale=1.0 / MD))
                A(ml4[:, 5, :], ml4[:, 4, :], ACT.Exp, scale=-0.5).then_inc(sem("h_rs"), 1)

            def mixT(t, p):
                act.wait_ge(sem("g_mx0"), t + 1)
                A(mT[:, 0:4, :], b2[:].rearrange("p (a b) -> p a b", a=4), copy).then_inc(sem("c_mx0"), 1)
                act.wait_ge(sem("g_mx1"), t + 1)
                A(mT[:, 4:8, :], b0[:].rearrange("p (a b) -> p a b", a=4), copy).then_inc(sem("c_mx1"), 1)

            def proj(t, p):
                act.wait_ge(sem("x1_ok"), t + 1)
                act.wait_ge(sem("c_delta"), t + 1)
                if isinstance(t, int) and t in (NPT - 1, SAMPLE):
                    act.wait_ge(sem("state_ok"), 1 + (t == SAMPLE))
                st(A(b56[:], xr[:], ACT.Square, accum_out=nr[:, 4:5]))
                st(A(nr[:, 5:6], nr[:, 4:5], ACT.Ln, bias=eps_c[:, 0:1], scale=1.0 / D))
                A(nr[:, 6:7], nr[:, 5:6], ACT.Exp, scale=-0.5).then_inc(sem("rstd2"), 1)

            def route_hT(t, p):
                for i, bank in ((0, b0), (1, b1)):
                    act.wait_ge(sem(f"g_hT{i}"), t + 1)
                    A(mT[:, 4 * i:4 * i + 4, :], bank[:].rearrange("p (a b) -> p a b", a=4), copy).then_inc(sem(f"c_hT{i}"), 1)

            def route(t, p):
                act.wait_ge(sem("g_max"), t + 1)
                A(rc[:, 4:8], lg8[:, 0:NG], ACT.Exp, bias=rc[:, 0:1], accum_out=rc[:, 1:2]).then_inc(sem("g_exp"), 1)
                act.wait_ge(sem("e_dif"), t + 1)
                A(rc[:, 10:11], rc[:, 9:10], ACT.Exp).then_inc(sem("e_exp"), 1)

            act.wait_ge(sem("const_in"), 16 * 21)
            act.wait_ge(sem("init_ok"), 1)
            def turn(t, p):
                if has(t - 1):
                    kr(t - 1, 1 - p)
                    w_exp(t - 1, 1 - p)
                    probs(0)(t - 1, 1 - p)
                if has(t):
                    evac_q(t, p)
                if has(t - 1):
                    probs_t(0)(t - 1, 1 - p)
                if has(t):
                    evac_kv(t, p)
                if has(t - 1):
                    inter(t - 1, 1 - p)
                    probs(1)(t - 1, 1 - p)
                    mid(t - 1, 1 - p)
                if has(t):
                    evac_c(0, b1)(t, p)
                if has(t - 1):
                    probs_t(1)(t - 1, 1 - p)
                if has(t):
                    evac_c(1, b2)(t, p)
                    evac_vm(t, p)
                if has(t - 1):
                    mixT(t - 1, 1 - p)
                if has(t + 1):
                    norm(t + 1, 1 - p)
                if has(t):
                    prep(t, p)
                if has(t - 1):
                    proj(t - 1, 1 - p)
                if has(t):
                    gate(t, p)
                    evac_o(t, p)
                if has(t - 1):
                    route_hT(t - 1, 1 - p)
                    route(t - 1, 1 - p)
                if has(t):
                    sig_o(t, p)

            norm(0, 0)
            walk(act, turn, st, STEPS["act"])

            act.preload_act_table_set("silu_and_others")
            act.wait_ge(sem("cnt_ok"), 1)
            with act.Fori(0, NE) as e:
                n = act.value_load(cnt_i[0:1, 0, bass.ds(e, 1)], min_val=1, max_val=CAP)
                g0 = act.value_load(cnt_i[0:1, 1, bass.ds(e, 1)], min_val=0, max_val=NB)
                with act.Fori(0, n) as b:
                    for j in range(FT):
                        act.wait_ge(sem("gu"), FT * (g0 + b) + j + 1)
                        A(eT[:, j, :], (b2, b7)[j % 2][:, 0:P], ACT.Silu).then_inc(sem("ge"), 1)
                    act.wait_ge(sem("dn"), g0 + b + 1)
                    act.wait_ge(sem("row_st"), 16 * (g0 + b + 1))
                    A(yrow[:], b56[:], copy).then_inc(sem("ye"), 1)

            act.preload_act_table_set("natural_log_exp_and_others")

            def last_norm(t, k, n=P):
                act.wait_ge(sem("f_x"), t + 1)
                st(A(f_r[k][3][0:n, :], f_r[k][2][0:n, :], ACT.Square, accum_out=nr[0:n, 0:1]))
                st(A(nr[0:n, 1:2], nr[0:n, 0:1], ACT.Ln, bias=eps_c[0:n, 0:1], scale=1.0 / D))
                A(nr[0:n, 2:3], nr[0:n, 1:2], ACT.Exp, scale=-0.5).then_inc(sem("f_rs"), 1)

            start = st.n
            with act.Fori(0, NPT // 2) as i:
                st.base, st.n = 4 * i, start
                last_norm(2 * i, 0)
                last_norm(2 * i + 1, 1)
            st.base, st.n = 0, start + 4 * (NPT // 2)
            last_norm(SAMPLE, 0, DEC)

        @block.tensor
        def _(pe):
            mm = nc.tensor.matmul

            def tr(out, in_, n=P):
                return nc.tensor.transpose(out, in_, ident[0:n, 0:n])

            pe.wait_ge(sem("c_silu"), 1)
            for i in range(NADA):
                pe.wait_ge(sem(f"ada_in{i % 2}"), 16 * (i // 2 + 1))
                if past(i - 1):
                    pe.wait_ge(sem("ada_row"), i - 1)
                for k in range(KT):
                    last = mm((b0, b1)[i % 2][0:2, :], cs[:, k, :], ada[i % 2][:, k, :], start=k == 0, stop=k == KT - 1)
                last.then_inc(sem("ada_mm"), 1)
            pe.wait_ge(sem("const_in"), 16 * 21)
            for h in range(MH):
                last = tr(b34[:, h * P:(h + 1) * P], kw[:, h, :])
            tr(b34[:, 512:640], qT[:, 0, :]).then_inc(sem("g_state"), 1)

            def norm(t, p):
                pe.wait_ge(sem("xn_ok"), t + 1)
                if past(t):
                    pe.wait_ge(sem("c_gates"), t)
                if past(t - 1):
                    pe.wait_ge(sem("c_hT0"), t - 1)
                if isinstance(t, int) and t == 0:
                    pe.wait_ge(sem("ada_row"), NADA)
                for k in range(4):
                    last = tr(b0[:, k * P:(k + 1) * P], smf[:, k:D:KT])
                last.then_inc(sem("g_n0"), 1)
                if past(t):
                    pe.wait_ge(sem("c_vm"), t)
                if past(t - 1):
                    pe.wait_ge(sem("c_hT1"), t - 1)
                for k in range(4):
                    last = tr(b1[:, k * P:(k + 1) * P], smf[:, 4 + k:D:KT])
                last.then_inc(sem("g_n1"), 1)

            def rowgroup(name, bank, c0, n, free, back):
                def f(t, p):
                    pe.wait_ge(sem("c_n1"), t + 1)
                    if past(t + 1 - back):
                        pe.wait_ge(sem(free), t + 1 - back)
                    for k in range(KT):
                        last = mm(bank[:, 0:n], hT[:, k, :], w_in[:, k, c0:c0 + n], start=k == 0, stop=k == KT - 1)
                    last.then_inc(sem(name), 1)
                return f

            def colgroup(i, bank, free):
                def f(t, p):
                    pe.wait_ge(sem(free), t + 1)
                    for c in range(4):
                        for k in range(KT):
                            at = C0 + (4 * i + c) * P
                            last = mm(bank[:, c * P:(c + 1) * P], w_in[:, k, at:at + P], hT[:, k, :],
                                      start=k == 0, stop=k == KT - 1)
                    last.then_inc(sem(f"g_qk{i}"), 1)
                return f

            def gates(t, p):
                pe.wait_ge(sem("c_kv"), t + 1)
                for k in range(KT):
                    last = mm(b0[0:32 + MH, 0:P], w_in[:, k, I0:F0 + MH], hT[:, k, :], start=k == 0, stop=k == KT - 1)
                last.then_inc(sem("g_gates"), 1)

            def qk(t, p):
                pe.wait_ge(sem("rope_ok"), t + 1)
                if past(t):
                    pe.wait_ge(sem("c_ptd1"), t)
                if past(t):
                    pe.wait_ge(sem("c_pta1"), t)
                if isinstance(t, int) and t == 0:
                    pe.wait_ge(sem("c_state"), 1)
                for g in range(G):
                    tr(b34[:, g * P:(g + 1) * P], qkv[:, 2 * g:2 * g + 2, :].rearrange("p a b -> p (a b)"))
                tr(b34[:, 512:640], qkv[:, 8:10, :].rearrange("p a b -> p (a b)")).then_inc(sem("g_tk"), 1)

            def gate(t, p):
                pe.wait_ge(sem("diag_ok"), t + 1)
                pe.wait_ge(sem("c_o"), t + 1)
                mm(b7[:], negones[:], md, start=True, stop=True).then_inc(sem("g_negm"), 1)
                pe.wait_ge(sem("stk_ok"), t + 1)
                pe.wait_ge(sem("c_tk"), t + 1)
                tr(b34[:, 640:768], stk[:])
                mm(b34[:, 768:768 + MH], ones[0:MH, :], dd[:], start=True, stop=True).then_inc(sem("g_cols"), 1)

            def kr(t, p):
                pe.wait_ge(sem("silu_y"), t + 1)
                pe.wait_ge(sem("xn_ok"), upto(t + 2))
                if past(t):
                    pe.wait_ge(sem("rstd2"), t)
                if isinstance(t, int) and t == SAMPLE:
                    pe.wait_ge(sem("state_ok"), 1)
                for h in range(MH):
                    last = tr(b56[:, h * P:(h + 1) * P], y[:, MH + h, :])
                last.then_inc(sem("g_kr"), 1)
                for h in range(MH):
                    last = mm(b56[:, 512 + h * P:512 + (h + 1) * P], y[:, MH + h, :], y[:, h, :], start=True, stop=True)
                last.then_inc(sem("g_sc"), 1)

            def scores(j):
                def f(t, p):
                    if j == 0:
                        pe.wait_ge(sem("c_cols"), t + 1)
                    else:
                        pe.wait_ge(sem("c_inter"), t + 1)
                    kp = prev(t, p, kT, kTs)
                    r = slice(HD * j, HD * j + HD)
                    for g in range(G):
                        mm(b34[:, g * 256:g * 256 + P], qT[r, g, :], kp[r, :], start=True, stop=True)
                        last = mm(b34[:, g * 256 + P:g * 256 + 256], qT[r, g, :], kT[p][r, :], start=True, stop=True)
                    last.then_inc(sem(f"g_s{j}"), 1)
                return f

            def intra(t, p):
                pe.wait_ge(sem("c_T"), t + 1)
                pe.wait_ge(sem("c_kw"), t + 1)
                for h in range(MH):
                    last = mm(head2(b56, h), wT[:, h, :], vmo[:, h, :], start=True, stop=True)
                last.then_inc(sem("g_intra"), 1)

            def turned(j):
                def f(t, p):
                    pe.wait_ge(sem(f"probs{j}"), t + 1)
                    for half in range(2):
                        for g in range(G):
                            last = tr(b34[:, half * 512 + g * P:half * 512 + (g + 1) * P], sm[:, g, half * P:(half + 1) * P])
                    last.then_inc(sem(f"g_pt{j}"), 1)
                return f

            def pv(j):
                def f(t, p):
                    pe.wait_ge(sem(f"c_ptd{j}"), t + 1)
                    pe.wait_ge(sem(f"c_pta{j}"), t + 1)
                    pe.wait_ge(sem("vk_ok"), t + 1)
                    vp = prev(t, p, vk, vs)
                    for g in range(G):
                        at = j * 256 + g * HD
                        mm(b7[:, at:at + HD], pT[:, 0, g, :], vp[:, j, :], start=True, stop=False)
                        last = mm(b7[:, at:at + HD], pT[:, 1, g, :], vk[p][:, j, :], start=False, stop=True)
                    last.then_inc(sem(f"g_pv{j}"), 1)
                return f

            def inter(t, p):
                C = C_s if isinstance(t, int) and t == SAMPLE else C_p
                if past(t):
                    pe.wait_ge(sem("c_delta"), t)
                pe.wait_ge(sem("c_ptd0"), t + 1)
                pe.wait_ge(sem("c_pta0"), t + 1)
                for h in range(MH):
                    last = mm(head2(b34, h), y[:, h, :], C[:, h, :], start=True, stop=True)
                last.then_inc(sem("g_inter"), 1)

            def delta(t, p):
                C = C_s if isinstance(t, int) and t == SAMPLE else C_p
                pe.wait_ge(sem("c_num"), t + 1)
                for h in range(MH):
                    last = mm(head2(b56, h), kw[:, h, :], vmo[:, h, :], start=True, stop=True)
                last.then_inc(sem("g_delta"), 1)
                if isinstance(t, int) and t in (NPT - 1, SAMPLE):
                    pe.wait_ge(sem("c_delta"), t + 1)
                    for h in range(MH):
                        last = tr(b56[:, h * P:(h + 1) * P], C[:, h, 0:MD])
                    last.then_inc(sem("g_stout"), 1)

            def mixT(t, p):
                pe.wait_ge(sem("mixed_h"), t + 1)
                pe.wait_ge(sem("att1"), t + 1)
                pe.wait_ge(sem("c_qk1"), upto(t + 2))
                for k in range(4):
                    last = tr(b2[:, k * P:(k + 1) * P], mix[:, k:D:KT])
                last.then_inc(sem("g_mx0"), 1)
                pe.wait_ge(sem("c_gates"), upto(t + 2))
                for k in range(4):
                    last = tr(b0[:, k * P:(k + 1) * P], mix[:, 4 + k:D:KT])
                last.then_inc(sem("g_mx1"), 1)

            def proj(t, p):
                pe.wait_ge(sem("c_mx1"), t + 1)
                pe.wait_ge(sem("c_vm"), upto(t + 2))
                for i, bank in ((0, b1), (1, b2)):
                    for k in range(KT):
                        last = mm(bank[:], mT[:, k, :], w_out[:, k, i * 512:(i + 1) * 512], start=k == 0, stop=k == KT - 1)
                    last.then_inc(sem(f"g_pr{i}"), 1)

            def route(t, p):
                pe.wait_ge(sem("h2"), t + 1)
                for i, bank in ((0, b0), (1, b1)):
                    for k in range(4):
                        last = tr(bank[:, k * P:(k + 1) * P], mix[:, 4 * i + k:D:KT])
                    last.then_inc(sem(f"g_hT{i}"), 1)
                pe.wait_ge(sem("c_hT1"), t + 1)
                for k in range(KT):
                    last = mm(b2[:, 0:NG + NE], mT[:, k, :], w_r[:, k, :], start=k == 0, stop=k == KT - 1)
                last.then_inc(sem("g_lg"), 1)

            def rank(t, p):
                pe.wait_ge(sem("M_ok"), t + 1)
                mm(b2[:, 64:64 + NE], lower[:], oh[:, 2, :], start=True, stop=False)
                mm(b2[:, 64:64 + NE], ones[:], Msum[:], start=False, stop=True).then_inc(sem("g_rank"), 1)

            pe.wait_ge(sem("win_in"), 16 * KT)
            pe.wait_ge(sem("wout_in"), 16)
            def turn(t, p):
                if has(t - 1):
                    qk(t - 1, 1 - p)
                    gate(t - 1, 1 - p)
                    kr(t - 1, 1 - p)
                    scores(0)(t - 1, 1 - p)
                if has(t):
                    rowgroup("g_q", b2, Q0, 512, "c_rank", 2)(t, p)
                if has(t - 1):
                    intra(t - 1, 1 - p)
                    turned(0)(t - 1, 1 - p)
                if has(t):
                    rowgroup("g_kv", b0, K0, 256, "c_n0", 0)(t, p)
                if has(t - 1):
                    pv(0)(t - 1, 1 - p)
                    inter(t - 1, 1 - p)
                if has(t):
                    gates(t, p)
                if has(t - 1):
                    scores(1)(t - 1, 1 - p)
                    delta(t - 1, 1 - p)
                if has(t):
                    colgroup(0, b1, "c_n1")(t, p)
                if has(t - 1):
                    turned(1)(t - 1, 1 - p)
                if has(t):
                    colgroup(1, b2, "c_q")(t, p)
                if has(t - 1):
                    pv(1)(t - 1, 1 - p)
                if has(t):
                    rowgroup("g_vm", b1, VM0, 512, "c_qk0", 0)(t, p)
                if has(t - 1):
                    mixT(t - 1, 1 - p)
                    proj(t - 1, 1 - p)
                if has(t):
                    rowgroup("g_o", b7, O0, 512, "att1", 1)(t, p)
                if has(t - 1):
                    route(t - 1, 1 - p)
                if has(t + 1):
                    norm(t + 1, 1 - p)
                if has(t - 1):
                    rank(t - 1, 1 - p)

            norm(0, 0)
            walk(pe, turn)

            pe.wait_ge(sem("Msum_ok"), NT)
            pe.wait_ge(sem("c_rank"), NT)
            mm(b2[:, 0:NE], ones[:], Msum[:], start=True, stop=True).then_inc(sem("g_cnt"), 1)
            pe.wait_ge(sem("lists_in"), 16 * 5)
            for j in range(5):
                n = min(P, NB - j * P)
                last = tr(b34[:, j * P:j * P + n], lists[0:n, j, :], n)
                if j == 0:
                    last.then_inc(sem("g_x1"), 1)
            last.then_inc(sem("g_lists"), 1)
            pe.wait_ge(sem("cnt_ok"), 1)
            pe.wait_ge(sem("idx_ok"), 1)

            def expert(e, k, i):
                w_g, w_u = ([half for piece in we[k][q] for half in (piece[:, 0:FE], piece[:, FE:D])] for q in range(2))
                w_g, w_u = ([z.rearrange("p (m j) -> p m j", j=FT) for z in w] for w in (w_g, w_u))
                w_d = we[k][2]
                n = pe.value_load(cnt_i[0:1, 0, bass.ds(e, 1)], min_val=1, max_val=CAP)
                g0 = pe.value_load(cnt_i[0:1, 1, bass.ds(e, 1)], min_val=0, max_val=NB)
                pe.wait_ge(sem(f"we_in{k}"), WE_IN[k] * (i + 1))
                apart(pe)
                with pe.Fori(0, n) as b:
                    g = g0 + b
                    pe.wait_ge(sem("gath"), 16 * (g + 1))
                    for q, bank in ((0, b0), (1, b1)):
                        for c in range(4):
                            last = tr(bank[:, c * P:(c + 1) * P], xg[:, 4 * q + c:D:KT])
                        last.then_inc(sem(f"g_x{q}"), 1)
                    pe.wait_ge(sem("c_x"), g + 1)
                    for j in range(FT):
                        if j >= 2:
                            pe.wait_ge(sem("a_ok"), FT * g + j - 1)
                        for q, wt in ((0, w_g), (1, w_u)):
                            bank, at = (b2, b7)[j % 2], q * P
                            for c in range(KT):
                                last = mm(bank[:, at:at + P], wt[c][:, :, j], xT[:, c, :], start=c == 0, stop=c == KT - 1)
                        last.then_inc(sem("gu"), 1)
                    pe.wait_ge(sem("ye"), g + 1)
                    for j in range(FT):
                        pe.wait_ge(sem("a_ok"), FT * g + j + 1)
                        for q in range(2):
                            last = mm(b56[:, q * 512:(q + 1) * 512], aT[:, j, :], w_d[j][:, q * 512:(q + 1) * 512],
                                      start=j == 0, stop=j == FT - 1)
                    last.then_inc(sem("dn"), 1)

            with pe.Fori(0, NE // 3) as i:
                for k in range(3):
                    expert(3 * i + k, k, i)
            for k in range(NE % 3):
                expert(NE // 3 * 3 + k, k, NE // 3)

        @block.vector
        def _(dve):
            st = Steps(dve, sem("dve_step"))
            v = nc.vector

            def bc(ap, shape):
                return ap.rearrange("p (a c) -> p a c", c=1).broadcast_to(shape)

            v.memset(cT[:], 0.0)
            v.memset(stk[:], 0.0)
            v.memset(Msum[:], 0.0)
            v.memset(C_p[:], 0.0)
            v.memset(m_st[1][:], 0.0)
            v.memset(lg8[:], -3e38)
            v.memset(vmo[:, :, MD:MD + 1], 1.0)
            v.memset(ones[:], 1.0)
            v.memset(negones[:], -1.0)
            v.memset(one_c[:], 1.0)
            v.memset(eps_c[:], EPS).then_inc(sem("init_ok"), 1)
            dve.wait_ge(sem("c_exp"), 1)
            st(v.tensor_scalar(cs[:], cs[:], 1.0, None, ALU.add))
            st(v.reciprocal(cs[:], cs[:]))
            v.tensor_tensor(cs[:], cc[:], cs[:], ALU.mult).then_inc(sem("c_silu"), 1)
            dve.wait_ge(sem("small_in"), 16 * (4 + NADA))
            gm, gf = (z[:, :, :].rearrange("p a b -> p (a b)") for z in (mT, hT))
            for i in range(NADA):
                buf = (yf, smf, xr, mix, row_gate, row_g2)[i // 2]
                r = buf[0:2, (i % 2) * 512:(i % 2) * 512 + 512]
                dve.wait_ge(sem("ada_mm"), i + 1)
                out = v.tensor_tensor(r, (b0, b1)[i % 2][0:2, :], r, ALU.add)
                if i // 2 in (1, 4):
                    st(out)
                    g_ = (gm if i // 2 == 1 else gf)[0:2, (i % 2) * 512:(i % 2) * 512 + 512]
                    out = v.scalar_tensor_tensor(out=r, in0=r, scalar=1.0, in1=g_, op0=ALU.add, op1=ALU.mult)
                out.then_inc(sem("ada_row"), 1)
            dve.wait_ge(sem("g_state"), 1)
            v.tensor_copy(C_s[:, :, 0:MD], b34[:, 0:512].rearrange("p (a b) -> p a b", a=MH))
            v.tensor_copy(kTs[:], b34[:, 512:640]).then_inc(sem("c_state"), 1)
            dve.wait_ge(sem("const_in"), 16 * 21)

            def norm(t, p):
                s_ = 1 if isinstance(t, int) and t == SAMPLE else 0
                dve.wait_ge(sem("modc_in"), 16 * 4)
                if past(t):
                    dve.wait_ge(sem("g_o"), t)
                for i, bank in ((0, b0), (1, b1)):
                    dve.wait_ge(sem(f"g_n{i}"), t + 1)
                    for c in range(4):
                        k = 4 * i + c
                        last = v.tensor_scalar(hT[:, k, :], bank[:, c * P:(c + 1) * P], mixc[:, s_, 0, k:k + 1],
                                               mixc[:, s_, 1, k:k + 1], ALU.mult, ALU.add)
                    last.then_inc(sem(f"c_n{i}"), 1)

            def gates_evac(t, p):
                dve.wait_ge(sem("g_gates"), t + 1)
                v.tensor_scalar(gr[:, 0, :], b0[0:MH, 0:P], b_i[:, 0:1], None, ALU.add)
                v.tensor_scalar(gr[:, 1, :], b0[32:32 + MH, 0:P], b_f[:, 0:1], None, ALU.add).then_inc(sem("c_gates"), 1)

            def qk(t, p):
                dve.wait_ge(sem("g_tk"), t + 1)
                v.tensor_copy(qT[:], b34[:, 0:512].rearrange("p (a b) -> p a b", a=G))
                v.tensor_copy(kT[p][:], b34[:, 512:640]).then_inc(sem("c_tk"), 1)

            def prep(t, p):
                dve.wait_ge(sem("c_qk0"), t + 1)
                dve.wait_ge(sem("c_qk1"), t + 1)
                if past(t):
                    dve.wait_ge(sem("g_inter"), t)
                for c in range(KT):
                    last = v.tensor_scalar(y[:, c, :], cT[:, c, CW - 1:CW - 1 + P], taps[:, CW - 1, c:c + 1],
                                           taps[:, CW, c:c + 1], ALU.mult, ALU.add)
                st(last)
                for j in range(CW - 1):
                    for c in range(KT):
                        last = v.scalar_tensor_tensor(out=y[:, c, :], in0=cT[:, c, j:j + P], scalar=taps[:, j, c:c + 1],
                                                      in1=y[:, c, :], op0=ALU.mult, op1=ALU.add)
                    if j < CW - 2:
                        st(last)
                last.then_inc(sem("conv_y"), 1)
                dve.wait_ge(sem("conv_y"), t + 1)
                if isinstance(t, int) and t >= NPT - 1:
                    at = P if t < NPT else DEC
                    st(v.tensor_copy(hist[t == SAMPLE][:].rearrange("p j c -> p c j"), cT[:, :, at:at + CW - 1]))
                new = hist_in[:].rearrange("p j c -> p c j") if isinstance(t, int) and t == NPT - 1 else cT[:, :, P:P + CW - 1]
                v.tensor_copy(cT[:, :, 0:CW - 1], new).then_inc(sem("conv_ok"), 1)
                dve.wait_ge(sem("silu_e"), t + 1)
                v.tensor_scalar(pTf, pTf, 1e18, 1.0, ALU.min, ALU.add).then_inc(sem("silu_1e"), 1)

            def silu(t, p):
                dve.wait_ge(sem("silu_s"), t + 1)
                v.scalar_tensor_tensor(out=yf[:, 0:512], in0=yf[:, 0:512], scalar=MD ** -0.5, in1=pTf[:, 0:512],
                                       op0=ALU.mult, op1=ALU.mult)
                v.tensor_tensor(yf[:, 512:1024], yf[:, 512:1024], pTf[:, 512:1024], ALU.mult).then_inc(sem("silu_y"), 1)

            def gate(t, p):
                sample = isinstance(t, int) and t == SAMPLE
                m_in = m_sa if sample else m_st[1 - p]
                dve.wait_ge(sem("c_gates"), t + 1)
                if past(t):
                    dve.wait_ge(sem("gate_e"), t)
                v.scalar_tensor_tensor(out=gr[:, 2, :], in0=gr[:, 1, :], scalar=-1.0, in1=gr[:, 1, :],
                                       op0=ALU.mult, op1=ALU.min).then_inc(sem("f_neg"), 1)
                dve.wait_ge(sem("f_log"), t + 1)
                st(v.scalar_tensor_tensor(out=gr[:, 1, :], in0=gr[:, 1, :], scalar=0.0, in1=gr[:, 2, :],
                                          op0=ALU.min, op1=ALU.subtract))
                if sample:
                    v.memset(gr[:, 0, DEC:P], -BIG)
                    st(v.memset(gr[:, 1, DEC:P], 0.0))
                st(v.tensor_tensor_scan(gr[:, 3, :], ones[0:MH, :], gr[:, 1, :], 0.0, ALU.mult, ALU.add))
                if past(t):
                    dve.wait_ge(sem("g_cols"), t)
                st(v.tensor_tensor(stk[0:MH, :], gr[:, 0, :], gr[:, 3, :], ALU.subtract))
                st(v.tensor_tensor_scan(gr[:, 4, :], ones[0:MH, :], stk[0:MH, :], m_in[:, 0:1], ALU.mult, ALU.max))
                st(v.tensor_tensor(gr[:, 5, :], gr[:, 3, :], gr[:, 4, :], ALU.add))
                v.tensor_copy(m_st[p][:], gr[:, 5, P - 1:P])
                v.tensor_scalar(g1c[:, 0:1], gr[:, 4, P - 1:P], -1.0, None, ALU.mult).then_inc(sem("gate_m"), 1)
                if past(t):
                    dve.wait_ge(sem("mixed_h"), t)
                v.tensor_tensor(md, gr[:, 4, :].rearrange("p (a b) -> p a b", a=1).broadcast_to([MH, MH, P]),
                                bc(ident[0:MH, 0:MH], [MH, MH, P]), ALU.mult).then_inc(sem("diag_ok"), 1)
                dve.wait_ge(sem("gate_e"), t + 1)
                v.tensor_scalar(dd[:], ident[0:MH, 0:MH], g1c[:, 1:2], None, ALU.mult).then_inc(sem("stk_ok"), 1)

            def columns(t, p):
                dve.wait_ge(sem("g_cols"), t + 1)
                v.tensor_copy(cols[:], b34[:, 640:768])
                v.tensor_copy(dec[:], b34[:, 768:768 + MH]).then_inc(sem("c_cols"), 1)

            def softmax(j):
                def f(t, p):
                    m = (0 if t == 0 else 2 if t == SAMPLE else 1) if isinstance(t, int) else 1
                    dve.wait_ge(sem(f"g_s{j}"), t + 1)
                    dve.wait_ge(sem("g_pt0" if j else "g_n1"), t + 1 if j else upto(t + 2))
                    st(v.tensor_tensor(sm[:], b34[:].rearrange("p (a b) -> p a b", a=4),
                                       amask[:, m:m + 1, :].broadcast_to([P, 4, 2 * P]), ALU.add))
                    st(v.tensor_reduce(at4[:, 0, :], sm[:], AX.X, ALU.max))
                    st(v.scalar_tensor_tensor(out=at4[:, 0, :], in0=at4[:, 0, :], scalar=HD ** -0.5,
                                              in1=sinks[:, 4 * j:4 * j + 4], op0=ALU.mult, op1=ALU.max))
                    v.tensor_scalar(at4[:, 1, :], at4[:, 0, :], -1.0, None, ALU.mult)
                    v.tensor_tensor(at4[:, 3, :], sinks[:, 4 * j:4 * j + 4], at4[:, 0, :], ALU.subtract).then_inc(sem(f"smax{j}"), 1)
                return f

            def weights(t, p):
                dve.wait_ge(sem("g_negm"), t + 1)
                v.tensor_tensor(wT[:], b7[:].rearrange("p (a b) -> p a b", a=MH),
                                cmask[:].rearrange("p (a b) -> p a b", a=1).broadcast_to([P, MH, P]), ALU.add).then_inc(sem("w_arg"), 1)

            def weights2(t, p):
                dve.wait_ge(sem("w_exp"), t + 1)
                dve.wait_ge(sem("g_sc"), t + 1)
                v.tensor_tensor(wT[:], b56[:, 512:1024].rearrange("p (a b) -> p a b", a=MH), wT[:], ALU.mult).then_inc(sem("c_T"), 1)

            def turned(j):
                def f(t, p):
                    dve.wait_ge(sem(f"g_pt{j}"), t + 1)
                    v.tensor_copy(pT[:, 0, :, :], b34[:, 0:512].rearrange("p (a b) -> p a b", a=4)).then_inc(sem(f"c_ptd{j}"), 1)
                return f

            def attend(j):
                def f(t, p):
                    dve.wait_ge(sem(f"probs{j}"), t + 1)
                    st(v.tensor_tensor(at4[:, 4, :], at4[:, 2, :], at4[:, 3, :], ALU.add))
                    st(v.reciprocal(at4[:, 4, :], at4[:, 4, :]))
                    dve.wait_ge(sem(f"g_pv{j}"), t + 1)
                    if j == 0:
                        if past(32 * t):
                            dve.wait_ge(sem("st_done"), 32 * t)
                        if past(t):
                            dve.wait_ge(sem("g_hT1"), t)
                    v.tensor_tensor(mix[:, 256 * j:256 * j + 256].rearrange("p (a b) -> p a b", a=G),
                                    b7[:, 256 * j:256 * j + 256].rearrange("p (a b) -> p a b", a=G),
                                    bc(at4[:, 4, :], [P, G, HD]), ALU.mult).then_inc(sem(f"att{j}"), 1)
                return f

            def inter(t, p):
                C = C_s if isinstance(t, int) and t == SAMPLE else C_p
                dve.wait_ge(sem("g_intra"), t + 1)
                dve.wait_ge(sem("c_inter"), t + 1)
                for i in range(2):
                    part = num[:, 2 * i:2 * i + 2, :]
                    last = v.tensor_tensor(part, b56[:, 512 * i:512 * i + 2 * (MD + 1)].rearrange("p (a b) -> p a b", a=2), part, ALU.add)
                last.then_inc(sem("c_num"), 1)

            def delta(t, p):
                C = C_s if isinstance(t, int) and t == SAMPLE else C_p
                dve.wait_ge(sem("g_delta"), t + 1)
                for h in range(MH):
                    last = v.scalar_tensor_tensor(out=C[:, h, :], in0=C[:, h, :], scalar=dec[:, h:h + 1], in1=head2(b56, h),
                                                  op0=ALU.mult, op1=ALU.add)
                last.then_inc(sem("c_delta"), 1)
                if isinstance(t, int) and t in (NPT - 1, SAMPLE):
                    dve.wait_ge(sem("g_stout"), 1 + (t == SAMPLE))
                    if t == SAMPLE:
                        dve.wait_ge(sem("state_out"), 48)
                    v.tensor_copy(kw[:], b56[:, 0:512].rearrange("p (a b) -> p a b", a=MH)).then_inc(sem("state_ok"), 1)

            def mid(t, p):
                dve.wait_ge(sem("c_num"), t + 1)
                st(v.scalar_tensor_tensor(out=ml4[:, 0, :], in0=num[:, :, MD], scalar=-1.0, in1=num[:, :, MD],
                                          op0=ALU.mult, op1=ALU.max))
                st(v.tensor_tensor(ml4[:, 0, :], ml4[:, 0, :], cols[:, 96:96 + MH], ALU.max))
                st(v.reciprocal(ml4[:, 0, :], ml4[:, 0, :]))
                st(v.tensor_tensor(ml4[:, 1, :], ml4[:, 0, :], ml4[:, 0, :], ALU.mult))
                dve.wait_ge(sem("h_sq"), t + 1)
                v.tensor_tensor(ml4[:, 3, :], ml4[:, 1, :], ml4[:, 2, :], ALU.mult).then_inc(sem("h_ms"), 1)
                dve.wait_ge(sem("o_sig"), t + 1)
                v.tensor_tensor(og[:], og[:], g_mh[:], ALU.mult)
                dve.wait_ge(sem("h_rs"), t + 1)
                st(v.tensor_tensor(ml4[:, 6, :], ml4[:, 5, :], ml4[:, 0, :], ALU.mult))
                st(v.tensor_tensor(wT[:], num[:, :, 0:MD], bc(ml4[:, 6, :], [P, MH, MD]), ALU.mult))
                if past(32 * t):
                    dve.wait_ge(sem("st_done"), 32 * t)
                v.tensor_tensor(mix[:, 512:1024].rearrange("p (a b) -> p a b", a=MH), wT[:], og[:], ALU.mult).then_inc(sem("mixed_h"), 1)

            def out_gate(t, p):
                dve.wait_ge(sem("c_o"), t + 1)
                v.tensor_scalar(og[:], og[:], 1e18, 1.0, ALU.min, ALU.add).then_inc(sem("o_1e"), 1)

            def proj(t, p):
                sample = isinstance(t, int) and t == SAMPLE
                dve.wait_ge(sem("rows_in"), 16 * (6 if sample else 3))
                dve.wait_ge(sem("xr_in"), 16 * (t + 1))
                dve.wait_ge(sem("g_mx1"), t + 1)
                for i, bank in ((0, b1), (1, b2)):
                    h = slice(512 * i, 512 * i + 512)
                    dve.wait_ge(sem(f"g_pr{i}"), t + 1)
                    v.tensor_tensor(mix[:, h], bank[:], row_gate[:, h], ALU.mult).then_inc(sem(f"c_pr{i}"), 1)
                    dve.wait_ge(sem(f"c_pr{i}"), t + 1)
                    last = v.tensor_tensor(xr[:, h], xr[:, h], mix[:, h], ALU.add)
                last.then_inc(sem("x1_ok"), 1)
                dve.wait_ge(sem("rstd2"), t + 1)
                st(v.scalar_tensor_tensor(out=mix[:], in0=xr[:], scalar=nr[:, 6:7], in1=row_g2[:], op0=ALU.mult, op1=ALU.mult))
                v.tensor_tensor(mix[:], mix[:], row_s2[:], ALU.add).then_inc(sem("h2"), 1)

            def route(t, p):
                sample = isinstance(t, int) and t == SAMPLE
                io4, io32 = iotas[:, 0:NG], iotas[:, NG:NG + NE]
                dve.wait_ge(sem("g_lg"), t + 1)
                v.tensor_tensor(lg8[:, 0:NG], b2[:, 0:NG], b_r[:, 0:NG], ALU.add)
                st(v.tensor_tensor(le[:], b2[:, NG:NG + NE], b_r[:, NG:NG + NE], ALU.add))
                apart(dve)
                st(v.max(gm8[:], lg8[:]))
                v.tensor_scalar(rc[:, 0:1], gm8[:, 0:1], -1.0, None, ALU.mult).then_inc(sem("g_max"), 1)
                st(v.max_index(gi8[:], gm8[:], lg8[:]))
                st(v.tensor_copy(rc[:, 2:3], gi8[:, 0:1]))
                st(v.tensor_scalar(gmk[:, 0, :], io4, rc[:, 2:3], None, ALU.is_equal))
                st(v.tensor_scalar(gmk[:, 1, :], gmk[:, 0, :], -1.0, BIG, ALU.add, ALU.mult))
                l3 = le[:].rearrange("p (a b) -> p a b", a=NG)
                st(v.tensor_tensor(l3, l3, bc(gmk[:, 0, :], [P, NG, EPG]), ALU.mult))
                st(v.tensor_tensor(l3, l3, bc(gmk[:, 1, :], [P, NG, EPG]), ALU.add))
                apart(dve)
                st(v.max(lv8[:], le[:]))
                v.tensor_tensor(rc[:, 9:10], lv8[:, 1:2], lv8[:, 0:1], ALU.subtract).then_inc(sem("e_dif"), 1)
                st(v.max_index(li8[:], lv8[:], le[:]))
                st(v.tensor_copy(rc[:, 2:4], li8[:, 0:2]))
                v.tensor_scalar(oh[:, 0, :], io32, rc[:, 2:3], None, ALU.is_equal)
                st(v.tensor_scalar(oh[:, 1, :], io32, rc[:, 3:4], None, ALU.is_equal))
                m = v.tensor_tensor(oh[:, 2, :], oh[:, 0, :], oh[:, 1, :], ALU.add)
                if sample:
                    st(m)
                    m = v.tensor_scalar(oh[:, 2, :], oh[:, 2, :], padcol[:, 0:1], None, ALU.mult)
                m.then_inc(sem("M_ok"), 1)

            def rank(t, p):
                dve.wait_ge(sem("g_rank"), t + 1)
                v.tensor_tensor(Msum[:], Msum[:], oh[:, 2, :], ALU.add).then_inc(sem("Msum_ok"), 1)
                v.tensor_tensor(oh[:, 3, :], b2[:, 64:64 + NE], iotas[:, NG + NE:], ALU.add).then_inc(sem("c_rank"), 1)

            def slots(t, p):
                sample = isinstance(t, int) and t == SAMPLE
                dve.wait_ge(sem("g_exp"), t + 1)
                dve.wait_ge(sem("e_exp"), t + 1)
                st(v.tensor_scalar(rc[:, 11:12], rc[:, 10:11], 1.0, None, ALU.add))
                st(v.tensor_tensor(rc[:, 11:12], rc[:, 11:12], rc[:, 1:2], ALU.mult))
                st(v.reciprocal(rc[:, 12:13], rc[:, 11:12]))
                v.tensor_copy(gate_all[:, 0, one(t)], rc[:, 12:13])
                v.tensor_tensor(gate_all[:, 1, one(t)], rc[:, 12:13], rc[:, 10:11], ALU.mult)
                dve.wait_ge(sem("c_rank"), t + 1)
                for k in range(2):
                    st(v.tensor_tensor(oh[:, 4, :], oh[:, 3, :], oh[:, k, :], ALU.mult))
                    st(v.tensor_reduce(rc[:, 13 + k:14 + k], oh[:, 4, :], AX.X, ALU.add))
                if sample:
                    st(v.scalar_tensor_tensor(out=rc[:, 13:15], in0=rc[:, 13:15], scalar=padcol[:, 0:1], in1=padcol[:, 1:3],
                                              op0=ALU.mult, op1=ALU.add))
                if past(32 * t):
                    dve.wait_ge(sem("scat"), 32 * t)
                v.tensor_copy(dst[:], rc[:, 13:15]).then_inc(sem("dst_ok"), 1)

            def turn(t, p):
                if has(t - 1):
                    qk(t - 1, 1 - p)
                    columns(t - 1, 1 - p)
                    weights(t - 1, 1 - p)
                    softmax(0)(t - 1, 1 - p)
                    weights2(t - 1, 1 - p)
                if has(t - 2):
                    slots(t - 2, p)
                if has(t - 1):
                    turned(0)(t - 1, 1 - p)
                    attend(0)(t - 1, 1 - p)
                    inter(t - 1, 1 - p)
                if has(t):
                    gates_evac(t, p)
                if has(t - 1):
                    softmax(1)(t - 1, 1 - p)
                    delta(t - 1, 1 - p)
                    mid(t - 1, 1 - p)
                    turned(1)(t - 1, 1 - p)
                    attend(1)(t - 1, 1 - p)
                if has(t):
                    prep(t, p)
                if has(t - 1):
                    proj(t - 1, 1 - p)
                if has(t):
                    gate(t, p)
                    silu(t, p)
                if has(t - 1):
                    route(t - 1, 1 - p)
                if has(t + 1):
                    norm(t + 1, 1 - p)
                if has(t - 1):
                    rank(t - 1, 1 - p)
                if has(t):
                    out_gate(t, p)

            norm(0, 0)
            walk(dve, turn, st, STEPS["dve"])

            dve.wait_ge(sem("g_cnt"), 1)
            st(v.tensor_scalar(cnt_f[:, 0, :], b2[0:1, 0:NE], P - 1.0, None, ALU.add))
            st(v.tensor_copy(cnt_i[:, 0, :], cnt_f[:, 0, :]))
            st(v.tensor_scalar(cnt_i[:, 0, :], cnt_i[:, 0, :], 7, None, ALU.arith_shift_right))
            st(v.tensor_copy(cnt_f[:, 0, :], cnt_i[:, 0, :]))
            st(v.tensor_scalar(cnt_f[:, 0, :], cnt_f[:, 0, :], 1.0, None, ALU.max))
            st(v.tensor_tensor_scan(cnt_f[:, 1, :], ones[0:1, 0:NE], cnt_f[:, 0, :], 0.0, ALU.mult, ALU.add))
            st(v.tensor_tensor(cnt_f[:, 2, :], cnt_f[:, 1, :], cnt_f[:, 0, :], ALU.subtract))
            v.tensor_copy(cnt_i[:, 0, :], cnt_f[:, 0, :])
            v.tensor_copy(cnt_i[:, 2, :], cnt_f[:, 1, NE - 1:NE].broadcast_to([1, NE]))
            v.tensor_copy(cnt_i[:, 1, :], cnt_f[:, 2, :]).then_inc(sem("cnt_ok"), 1)
            dve.wait_ge(sem("g_lists"), 1)
            st(v.tensor_copy(sidx_all, b34[:, 0:NB]))
            st(v.tensor_scalar(smf[:, 0:NB], b34[:, 0:NB], float(NT * P), -float(NT * P), ALU.is_ge, ALU.mult))
            st(v.tensor_tensor(smf[:, 0:NB], b34[:, 0:NB], smf[:, 0:NB], ALU.add))
            st(v.tensor_scalar(num_f, smf[:, 0:NB], float(NT * P), -float(NT * P), ALU.is_ge, ALU.mult))
            dve.wait_ge(sem("rstd2"), NT)
            v.tensor_tensor(idx_all, smf[:, 0:NB], num_f, ALU.add).then_inc(sem("idx_ok"), 1)
            v.memset(yrow[:], 0.0).then_inc(sem("ye"), 1)
            dve.wait_ge(sem("cnt_ok"), 1)

            base = st.n
            with dve.Fori(0, NE) as e:
                n = dve.value_load(cnt_i[0:1, 0, bass.ds(e, 1)], min_val=1, max_val=CAP)
                g0 = dve.value_load(cnt_i[0:1, 1, bass.ds(e, 1)], min_val=0, max_val=NB)
                with dve.Fori(0, n) as b:
                    g = g0 + b
                    for i, bank in ((0, b0), (1, b1)):
                        dve.wait_ge(sem(f"g_x{i}"), g + 1 + i)
                        last = v.tensor_copy(xT[:, 4 * i:4 * i + 4, :], bank[:].rearrange("p (a b) -> p a b", a=4))
                    last.then_inc(sem("c_x"), 1)
                    for j in range(FT):
                        bank = (b2, b7)[j % 2]
                        q = FT * g + j
                        dve.wait_ge(sem("ge"), q + 1)
                        v.tensor_tensor(aT[:, j, :], bank[:, P:2 * P], eT[:, j, :], ALU.mult).then_inc(sem("a_ok"), 1)

            dve.wait_ge(sem("rows4_in"), 48)

            def last_rows(t, k, half, n=P):
                r0, r1, x1, out = (z[0:n, :] for z in f_r[k])
                gate5 = row_s2 if isinstance(t, int) and t == SAMPLE else row_gate
                dve.wait_ge(sem(f"x1_in{k}"), 48 * (half + 1))
                g_ = f_g[k]
                st(v.tensor_copy(g_[:], gate_all[:, :, one(t)].rearrange("p a b -> p (a b)")))
                st(v.tensor_scalar(r0, r0, g_[0:n, 0:1], None, ALU.mult))
                st(v.scalar_tensor_tensor(out=r0, in0=r1, scalar=g_[0:n, 1:2], in1=r0, op0=ALU.mult, op1=ALU.add))
                st(v.tensor_tensor(r0, r0, gate5[0:n, :], ALU.mult))
                v.tensor_tensor(x1, x1, r0, ALU.add).then_inc(sem("f_x"), 1)
                dve.wait_ge(sem("f_rs"), t + 1)
                v.scalar_tensor_tensor(out=out, in0=x1, scalar=nr[0:n, 2:3], in1=row_g2[0:n, :], op0=ALU.mult, op1=ALU.mult)\
                    .then_inc(sem("y_ok"), 1)

            start = st.n
            with dve.Fori(0, NPT // 2) as i:
                st.base, st.n = 8 * i, start
                last_rows(2 * i, 0, i)
                last_rows(2 * i + 1, 1, i)
            st.base, st.n = 0, start + 8 * (NPT // 2)
            last_rows(SAMPLE, 0, NPT // 2, DEC)


_INS = ["x", "c_both", "w_ada", "b_ada", "g_mix", "g_ffn", "w_in", "sinks", "taps", "b_ig", "b_fg", "g_mh", "w_out",
        "w_r", "b_r", "w_g", "w_u", "w_d", "g_final", "cache_k", "cache_v", "state_conv", "state_C", "state_n",
        "state_m", "c_ident", "c_cmask", "c_lower", "c_amask", "c_iotas", "c_tokid", "c_padcol", "c_trash", "rope"]


def kernel(**inp):
    import numpy as np
    import concourse.bacc as bacc
    from concourse.bass_utils import run_bass_kernel_spmd

    f = np.float32
    inp = {k: np.ascontiguousarray(v) for k, v in inp.items()}
    a = {}
    a["x"] = np.concatenate([inp["x_prompt"][0], inp["x_sample"][0], np.zeros((P - DEC, D), f)])
    a["c_both"] = np.stack([inp["c_prompt"][0], inp["c_sample"][0]], axis=1)
    a["w_ada"], a["b_ada"] = inp["w_ada"][0], inp["b_ada"][0]
    a["g_mix"], a["g_ffn"], a["g_final"] = inp["g_norm_mix"][0], inp["g_norm_ffn"][0], inp["g_final"]
    order = np.concatenate([np.arange(NH * HD).reshape(NKV, G, HD).transpose(1, 0, 2).ravel(), np.arange(NH * HD, inp["w_in"].shape[2])])
    a["w_in"] = inp["w_in"][0][:, order]
    a["w_in"] = np.insert(a["w_in"], [I0 + MH] * (32 - MH), 0.0, axis=1)
    a["sinks"], a["b_ig"], a["b_fg"] = inp["attn_sinks"][0], inp["b_igate"][0], inp["b_fgate"][0]
    a["taps"] = np.concatenate([inp["conv_w"][0], inp["conv_b"]]).reshape(CW + 1, KT, P).transpose(2, 0, 1)
    a["g_mh"], a["w_out"] = inp["g_mhnorm"][0], inp["w_out"][0]
    a["w_r"] = np.concatenate([inp["w_router_group"][0], inp["w_router_expert"][0]], axis=1)
    a["b_r"] = np.concatenate([inp["b_router_group"][0], inp["b_router_expert"][0]])
    a["w_g"], a["w_u"], a["w_d"] = inp["w_exp_gate"][0], inp["w_exp_up"][0], inp["w_exp_down"][0]
    a["cache_k"] = inp["cache_win_k"].reshape(P, NKV * HD)
    a["cache_v"] = inp["cache_win_v"].reshape(P, NKV * HD)
    a["state_conv"] = inp["state_conv"].reshape(CW - 1, KT, P).transpose(2, 0, 1)
    a["state_C"], a["state_n"], a["state_m"] = inp["state_C"][0, 0], inp["state_n"][0, 0], inp["state_m"][0, 0]
    i = np.arange(P)
    a["c_ident"] = np.eye(P, dtype=f)
    a["c_cmask"] = np.where(i[:, None] <= i[None, :], 0.0, -BIG).astype(f)
    a["c_lower"] = (i[:, None] < i[None, :]).astype(f)
    key = np.arange(2 * P)[None, :]
    q = i[:, None]
    band = (key // CHUNK >= q // CHUNK) & (key // CHUNK <= q // CHUNK + 2)
    a["c_amask"] = np.stack([np.where(m, 0.0, -BIG) for m in
                             (band & (key >= P), band, np.broadcast_to(key < P + DEC, band.shape))], axis=1).astype(f)
    a["c_iotas"] = np.tile(np.concatenate([np.arange(NG), np.arange(NE), np.arange(NE) * CAP * P]), (P, 1)).astype(f)
    a["c_tokid"] = (i[:, None] + P * np.arange(NT)[None, :]).astype(f)
    a["c_trash"] = np.tile(TRASH + i, (P, 1)).astype(f)
    pad = (i >= DEC).astype(f)
    a["c_padcol"] = np.stack([1 - pad, pad * (SLOTS + i), pad * (SLOTS + P + i)], axis=1).astype(f)
    pos = np.concatenate([np.arange(SEQ), PAST + np.arange(P)]).astype(f)
    freq = (f(500000.0) ** (-np.arange(0, ROT, 2, dtype=f) / f(ROT))).astype(f)
    ang = pos[:, None] * freq[None, :]
    c, s = np.cos(ang), np.sin(ang)
    a["rope"] = np.concatenate([c, c, -s, s], axis=1).astype(f)

    nc = bacc.Bacc("TRN2", target_bir_lowering=False, num_devices=1)
    arrays, ins, outs = {}, {}, {}
    for name in _INS:
        arrays[f"in_{name}"] = np.ascontiguousarray(a[name])
        ins[name] = nc.dram_tensor(f"in_{name}", arrays[f"in_{name}"].shape, F32, kind="ExternalInput").ap()
    shapes = {"y_p": (SEQ, D), "y_s": (DEC, D)}
    for s_ in "ps":
        shapes |= {f"k_{s_}": (P, NKV * HD), f"v_{s_}": (P, NKV * HD), f"conv_{s_}": (P, CW - 1, KT),
                   f"C_{s_}": (MH, MD, MD), f"n_{s_}": (MH, MD), f"m_{s_}": (MH,)}
    for name, shape in shapes.items():
        outs[name] = nc.dram_tensor(f"out_{name}", shape, F32, kind="ExternalOutput").ap()
    build(nc, ins, outs)
    r = run_bass_kernel_spmd(nc, [arrays], core_ids=[0]).results[0]
    got = {name: r[f"out_{name}"] for name in shapes}
    res = [got["y_p"].reshape(1, SEQ, D), got["y_s"].reshape(1, DEC, D)]
    for s_ in "ps":
        res += [got[f"k_{s_}"].reshape(1, 1, P, NKV, HD), got[f"v_{s_}"].reshape(1, 1, P, NKV, HD),
                got[f"conv_{s_}"].transpose(1, 2, 0).reshape(1, 1, CW - 1, 2 * MH * MD),
                got[f"C_{s_}"].reshape(1, 1, MH, MD, MD), got[f"n_{s_}"].reshape(1, 1, MH, MD), got[f"m_{s_}"].reshape(1, 1, MH)]
    return tuple(res)
```

```python
from contextlib import ExitStack

import concourse.bass as bass
from concourse import mybir

F32 = mybir.dt.float32
I32 = mybir.dt.int32
U32 = mybir.dt.uint32
ALU = mybir.AluOpType
ACT = mybir.ActivationFunctionType
AX = mybir.AxisListType

P = 128
D = 1024
KT = D // P
SEQ, DEC, PAST = 2048, 64, 4096
NPT = SEQ // P
NT = NPT + 1
SAMPLE = NT - 1
CHUNK = 64
HD = 64
NH, NKV = 8, 2
G = NH // NKV
ROT = HD // 4
MH, MD = 4, 128
CW = 4
NG, EPG = 4, 8
NE = NG * EPG
FE = D // 2
FT = FE // P
CAP = NT
NB = NE * CAP
SLOTS = NB * P
TRASH = 2 * NT * P
NB4 = 4
EPS = 1e-6
BIG = 1e30
Q0, K0, C0, VM0, I0, F0, O0, DIN = 0, 512, 768, 1792, 2304, 2336, 2340, 2852
NADA = 6 * D // 512

STEPS = {"dve": 92, "act": 18, "pool": 6}


class Steps:

    def __init__(self, eng, s):
        self.eng, self.s, self.base, self.n = eng, s, 0, 0

    def __call__(self, ins):
        self.n += 1
        ins.then_inc(self.s, 1)
        self.eng.wait_ge(self.s, self.base + self.n)


def has(t):
    return not isinstance(t, int) or 0 <= t < NT


def walk(eng, turn, steps=None, per_turn=0):
    turn(0, 0)
    turn(1, 1)
    pairs = NPT // 2 - 2
    start = steps.n if steps else 0
    with eng.Fori(0, pairs) as i:
        if steps:
            steps.base, steps.n = i * per_turn, start
        turn(2 * i + 2, 0)
        turn(2 * i + 3, 1)
    if steps:
        if steps.n - start != per_turn:
            raise ValueError(f"{steps.s}: {steps.n - start} steps in a pair of turns, not {per_turn}")
        steps.base, steps.n = 0, start + pairs * per_turn
    turn(NPT - 2, 0)
    turn(NPT - 1, 1)
    turn(NPT, 0)
    turn(NT, 1)
    turn(NT + 1, 0)


def past(v):
    return not isinstance(v, int) or v > 0


def upto(v):
    return min(v, NT) if isinstance(v, int) else v


def build(nc, a, o):
    with ExitStack() as ctx:
        def sb(name, shape, dt=F32):
            return ctx.enter_context(nc.sbuf_tensor(name, shape, dt))

        def dram(name, shape):
            return nc.dram_tensor(name, shape, F32, kind="Internal").ap()

        S = {}

        def sem(name):
            if name not in S:
                S[name] = ctx.enter_context(nc.semaphore(name))
            return S[name]

        def apart(eng):
            eng.sem_inc(sem("apart"), 1)

        mods_d = dram("mods_d", [2, 6 * D])
        x1_d = dram("x1_d", [NT * P, D])
        h2_d = dram("h2_d", [NT * P, D])
        list_d = dram("list_d", [SLOTS + 2 * P, 1])
        rows_d = dram("rows_d", [TRASH + P, D])

        big = sb("big", [P, KT * DIN + KT * D])
        w_in = big[:, 0:KT * DIN].rearrange("p (k n) -> p k n", k=KT)
        w_out = big[:, KT * DIN:KT * DIN + KT * D].rearrange("p (k n) -> p k n", k=KT)
        ada = [big[:, KT * DIN + i * KT * 512:KT * DIN + (i + 1) * KT * 512].rearrange("p (k n) -> p k n", k=KT)
               for i in range(2)]
        WE = KT * FE
        ident = sb("ident", [P, P])
        cmask = sb("cmask", [P, P])
        lower = sb("lower", [P, P])
        ones = sb("ones", [P, P])
        negones = sb("negones", [MH, P])
        amask = sb("amask", [P, 3, 2 * P])
        iotas = sb("iotas", [P, NG + 2 * NE])
        tokid = sb("tokid", [P, NT])
        padcol = sb("padcol", [P, 3])
        eps_c = sb("eps_c", [P, 1])
        one_c = sb("one_c", [P, 1])
        w_r = sb("w_r", [P, KT, NG + NE])
        b_r = sb("b_r", [P, NG + NE])
        taps = sb("taps", [P, CW + 1, KT])
        g_mh = sb("g_mh", [P, MH, MD])
        sinks = sb("sinks", [P, NH])
        b_i = sb("b_i", [MH, 1])
        b_f = sb("b_f", [MH, 1])
        mixc = sb("mixc", [P, 2, 2, KT])
        cc = sb("cc", [P, KT, 2])
        cs = sb("cs", [P, KT, 2])
        row_gate = sb("row_gate", [P, D])
        row_g2 = sb("row_g2", [P, D])
        row_s2 = sb("row_s2", [P, D])
        xr = sb("xr", [P, D])
        rope_t = sb("rope_t", [P, 2 * ROT])
        hT = sb("hT", [P, KT, P])
        qkv = sb("qkv", [P, 12, HD])
        vmo = sb("vmo", [P, MH, MD + 1])
        og = sb("og", [P, MH, MD])
        cT = sb("cT", [P, KT, CW - 1 + P])
        hist = [sb("hist_p", [P, CW - 1, KT]), sb("hist_s", [P, CW - 1, KT])]
        hist_in = sb("hist_in", [P, CW - 1, KT])
        y = sb("y", [P, KT, P])
        sm = sb("sm", [P, 4, 2 * P])
        smf = sm[:, :, :].rearrange("p a b -> p (a b)")
        yf = y[:, :, :].rearrange("p a b -> p (a b)")
        rt = sb("rt", [P, 2, 10, ROT])
        qT = sb("qT", [P, G, P])
        kT = [sb("kT0", [P, P]), sb("kT1", [P, P])]
        kTs = sb("kTs", [P, P])
        vk = [sb("vk0", [P, NKV, HD]), sb("vk1", [P, NKV, HD])]
        vs = sb("vs", [P, NKV, HD])
        pT = sb("pT", [P, 2, 4, P])
        pTf = pT[:, :, :, :].rearrange("p a b c -> p (a b c)")
        wT = sb("wT", [P, MH, P])
        kw = sb("kw", [P, MH, MD])
        C_p = sb("C_pr", [P, MH, MD + 1])
        C_s = sb("C_sa", [P, MH, MD + 1])
        mix = sb("mix", [P, D])
        mT = sb("mT", [P, KT, P])
        num = sb("num", [P, MH, MD + 1])
        md = num[0:MH, :, 0:P]
        gr = sb("gr", [MH, 6, P])
        stk = sb("stk", [P, P])
        cols = sb("cols", [P, P])
        dec = sb("dec", [P, MH])
        dd = sb("dd", [MH, MH])
        m_st = [sb("m_st0", [MH, 1]), sb("m_st1", [MH, 1])]
        m_sa = sb("m_sa", [MH, 1])
        g1c = sb("g1c", [MH, 2])
        at4 = sb("at4", [P, 8, 4])
        ml4 = sb("ml4", [P, 8, 4])
        nr = sb("nr", [P, 8])
        lg8 = sb("lg8", [P, 8])
        le = sb("le", [P, NE])
        gm8 = sb("gm8", [P, 8])
        gi8 = sb("gi8", [P, 8], U32)
        lv8 = sb("lv8", [P, 8])
        li8 = sb("li8", [P, 8], U32)
        rc = sb("rc", [P, 16])
        gmk = sb("gmk", [P, 2, NG])
        oh = sb("oh", [P, 5, NE])
        Msum = sb("Msum", [P, NE])
        dst = sb("dst", [P, 2], I32)
        gate_all = sb("gate_all", [P, 2, NT])
        tok_s = sb("tok_s", [P, 2])
        sidx_f = sb("sidx_f", [P, 1])
        sidx = sb("sidx", [P, 1], I32)
        sidx_n = sb("sidx_n", [P, 1], I32)
        cnt_f = sb("cnt_f", [1, 4, NE])
        cnt_i = sb("cnt_i", [1, 3, NE], I32)
        idx_all = yf[:, 0:NB].bitcast(I32)
        sidx_all = mT[:, :, :].rearrange("p a b -> p (a b)")[:, 0:NB].bitcast(I32)
        idx = sb("idx", [P, 1], I32)
        num_f = pT[:, :, :, :].rearrange("p a b c -> p (a b c)")[:, 0:NB]
        lists = smf[:, 0:5 * P].rearrange("p (a b) -> p a b", a=5)
        xg, xT, aT, yrow = xr, hT, qT, mix
        e_a = wT[:, :, :].rearrange("p a b -> p (a b)")
        pieces = [big[:, j * D:(j + 1) * D] for j in range(30)]
        pieces += [smf, cT[:, :, :].rearrange("p a b -> p (a b)")[:, 0:D], pTf, row_gate[:], row_g2[:], row_s2[:]]
        WE_IN = (48, 48, 16 * (1 + 3 + 4))
        NW = WE // D
        we = [[pieces[(3 * i + j) * NW:(3 * i + j + 1) * NW] for j in range(3)] for i in range(3)]
        f_r = [[big[:, (4 * i + j) * D:(4 * i + j + 1) * D] for j in range(4)] for i in range(NB4)]
        f_g = [sb(f"f_g{i}", [P, 2]) for i in range(NB4)]

        b0 = ctx.enter_context(nc.psum_tensor("b0", [P, 512], F32))
        b1 = ctx.enter_context(nc.psum_tensor("b1", [P, 512], F32))
        b2 = ctx.enter_context(nc.psum_tensor("b2", [P, 512], F32))
        b34 = ctx.enter_context(nc.psum_tensor("b34", [P, 1024], F32))
        b56 = ctx.enter_context(nc.psum_tensor("b56", [P, 1024], F32))
        b7 = ctx.enter_context(nc.psum_tensor("b7", [P, 512], F32))

        def row(ap):
            return ap.rearrange("(a n) -> a n", a=1)

        def rows(t):
            return slice(t * P, t * P + P) if isinstance(t, int) else bass.ds(t * P, P)

        def one(t):
            return slice(t, t + 1) if isinstance(t, int) else bass.ds(t, 1)

        def prev(t, p, own, sample):
            return sample if isinstance(t, int) and t in (0, SAMPLE) else own[1 - p]

        def head2(bank, h):
            at = (h // 2) * 512 + (h % 2) * (MD + 1)
            return bank[:, at:at + MD + 1]

        ctx.enter_context(nc.allow_non_contiguous_dma(reason="a few small columns"))
        block = ctx.enter_context(nc.Block())

        @block.sync
        def _(sp):
            def move(name, to, frm):
                sp.dma_start(to, frm).then_inc(sem(name), 16)

            move("c_in", cc[:], a["c_both"].rearrange("(p k) s -> p k s", k=KT))

            def mods_out(i):
                sp.wait_ge(sem("ada_row"), i + 1)
                buf = (yf, smf, xr, mix, row_gate, row_g2)[i // 2]
                move("mod1_out" if i < 4 else "mods_out", mods_d[:, i * 512:i * 512 + 512],
                     buf[0:2, (i % 2) * 512:(i % 2) * 512 + 512])

            def first_tile():
                sp.wait_ge(sem("mod1_out"), 16 * 4)
                move("x_in", smf, a["x"][0:P, :])
                for s_ in range(2):
                    for j, m in enumerate((1, 0)):
                        move("modc_in", mixc[:, s_, j, :],
                             mods_d[s_, m * D:(m + 1) * D].rearrange("(p k) -> p k", k=KT))

            for i in range(NADA):
                if past(i - 1):
                    sp.wait_ge(sem("ada_mm"), i - 1)
                move(f"ada_in{i % 2}", ada[i % 2],
                     a["w_ada"].rearrange("(p k) n -> p k n", k=KT)[:, :, i * 512:i * 512 + 512])
                if i >= 4:
                    move("win_in", w_in[:, i - 4, :], a["w_in"].rearrange("(p k) n -> p k n", k=KT)[:, i - 4, :])
                if i >= 2:
                    mods_out(i - 2)
                if i == 7:
                    first_tile()
            sp.wait_ge(sem("ada_mm"), NADA)
            move("wout_in", w_out, a["w_out"].rearrange("(p k) n -> p k n", k=KT))
            mods_out(NADA - 2)
            mods_out(NADA - 1)
            sp.wait_ge(sem("mods_out"), 16 * (NADA - 4))

            def modrow(to, s_, m, name="rows_in"):
                move(name, to[:], mods_d[s_:s_ + 1, m * D:(m + 1) * D].broadcast_to([P, D]))

            modrow(row_gate, 0, 2)
            modrow(row_s2, 0, 3)
            modrow(row_g2, 0, 4)

            def weights(e, k, which=(0, 1, 2)):
                for j in which:
                    name = ("w_g", "w_u", "w_d")[j]
                    src = a[name][e:e + 1] if isinstance(e, int) else a[name][bass.ds(e, 1), :, :]
                    src = src.rearrange("a (k p) n -> p (a k) n" if j == 2 else "a (p k) n -> p (a k) n", p=P)
                    rows_ = NW if j == 2 else KT
                    at = 0
                    while at < NW:
                        n = 1
                        first = (3 * k + j) * NW + at
                        while at + n < NW and first + n < 30:
                            n += 1
                        to = big[:, first * D:(first + n) * D] if first < 30 else pieces[first]
                        per = rows_ // NW
                        move(f"we_in{k}", to.rearrange("p (k n) -> p k n", k=n * per), src[:, at * per:(at + n) * per, :])
                        at += n

            def first_experts(t, p):
                if isinstance(t, int) and t == SAMPLE:
                    sp.wait_ge(sem("g_o"), NT)
                    weights(0, 0)
                    weights(1, 1, (0, 1))

            def load_x(t, p):
                if isinstance(t, int) and t == 0:
                    return
                if past(t):
                    sp.wait_ge(sem("g_n"), t)
                if past(t - 1):
                    sp.wait_ge(sem("g_pt1"), t - 1)
                move("x_in", smf, a["x"][rows(t), :])

            def load_rope(t, p):
                if past(t):
                    sp.wait_ge(sem("rope_ok"), t)
                move("rope_in", rope_t[:], a["rope"][rows(t), :])

            def load_xr(t, p):
                if past(32 * t):
                    sp.wait_ge(sem("st_done"), 32 * t)
                move("xr_in", xr[:], a["x"][rows(t), :])

            def windows(t, p):
                if isinstance(t, int) and t in (NPT - 1, SAMPLE):
                    s_, n = ("p", P) if t < NPT else ("s", DEC)
                    sp.wait_ge(sem("rope_ok"), t + 1)
                    sp.wait_ge(sem("c_kv"), t + 1)
                    move("kv_out", o[f"k_{s_}"][P - n:P, :], qkv[0:n, 8:10, :].rearrange("p a b -> p (a b)"))
                    move("kv_out", o[f"v_{s_}"][P - n:P, :], qkv[0:n, 10:12, :].rearrange("p a b -> p (a b)"))
                    if t == SAMPLE:
                        move("win_out", o["k_s"][0:P - n, :], a["cache_k"][n:P, :])
                        move("win_out", o["v_s"][0:P - n, :], a["cache_v"][n:P, :])
                    sp.wait_ge(sem("conv_ok"), t + 1)
                    move("win_out", o[f"conv_{s_}"], hist[t == SAMPLE][:])

            def states(t, p):
                if isinstance(t, int) and t in (NPT - 1, SAMPLE):
                    s_ = "p" if t < NPT else "s"
                    sp.wait_ge(sem("state_ok"), 1 + (t == SAMPLE))
                    move("state_out", o[f"C_{s_}"].rearrange("h v k -> v h k"), kw[:])
                    move("state_out", o[f"n_{s_}"].rearrange("h k -> k h"), (C_p, C_s)[t == SAMPLE][:, :, MD])
                    move("state_out", o[f"m_{s_}"].rearrange("(n a) -> n a", a=1), m_st[p][:])

            def stores(t, p):
                sp.wait_ge(sem("h2"), t + 1)
                move("st_done", x1_d[rows(t), :], xr[:])
                move("st_done", h2_d[rows(t), :], mix[:])
                if isinstance(t, int) and t == NPT - 1:
                    modrow(row_gate, 1, 2)
                    modrow(row_s2, 1, 3)
                    modrow(row_g2, 1, 4)

            def turn(t, p):
                if has(t - 1):
                    load_xr(t - 1, 1 - p)
                    windows(t - 1, 1 - p)
                    first_experts(t - 1, 1 - p)
                if has(t):
                    load_rope(t, p)
                if has(t - 1):
                    states(t - 1, 1 - p)
                if has(t + 1):
                    load_x(t + 1, 1 - p)
                if has(t - 1):
                    stores(t - 1, 1 - p)

            load_x(0, 0)
            walk(sp, turn)

            sp.wait_ge(sem("scat"), 32 * NT)
            sp.wait_ge(sem("h2"), NT)
            sp.wait_ge(sem("g_hT1"), NT)
            for j in range(5):
                n = min(P, NB - j * P)
                move("lists_in", lists[0:n, j, :], list_d[j * P * P:(j * P + n) * P, :].rearrange("(b s) a -> b (s a)", s=P))
            sp.wait_ge(sem("g_pr1"), NT)
            sp.wait_ge(sem("idx_ok"), 1)
            sp.wait_ge(sem("gath"), 32)
            weights(1, 1, (2,))
            weights(2, 2)
            sp.wait_ge(sem("cnt_ok"), 1)

            def used(e):
                return sp.value_load(cnt_i[0:1, 1, bass.ds(e + 1, 1)], min_val=0, max_val=NB)

            with sp.Fori(0, NE // 3 - 1) as i:
                for k in range(3):
                    done = used(3 * i + k)
                    sp.wait_ge(sem("dn"), done)
                    sp.wait_ge(sem("gath"), 16 * done + 32)
                    weights(3 * i + k + 3, k)
            for k in range(3):
                done = used(NE // 3 * 3 - 3 + k)
                sp.wait_ge(sem("dn"), done)
                if k < NE % 3:
                    sp.wait_ge(sem("gath"), 16 * done + 32)
                    weights(NE // 3 * 3 + k, k)
            modrow(row_gate, 0, 5, "rows4_in")
            modrow(row_s2, 1, 5, "rows4_in")
            move("rows4_in", row_g2[:], row(a["g_final"]).broadcast_to([P, D]))

            blocks = sp.value_load(cnt_i[0:1, 2, 0:1], min_val=0, max_val=NB)
            sp.wait_ge(sem("dn"), blocks)
            sp.wait_ge(sem("row_st"), 16 * blocks + 32)

            def out_tile(t, k, turn):
                n = DEC if isinstance(t, int) and t == SAMPLE else P
                again = not (isinstance(turn, int) and turn == 0)
                if again:
                    sp.wait_ge(sem("f_x"), t - NB4 + 1)
                r = slice(t * P, t * P + n) if isinstance(t, int) else bass.ds(t * P, P)
                r1 = slice(NT * P + t * P, NT * P + t * P + n) if isinstance(t, int) else bass.ds(NT * P + t * P, P)
                move(f"x1_in{k}", f_r[k][0][0:n, :], rows_d[r, :])
                move(f"x1_in{k}", f_r[k][1][0:n, :], rows_d[r1, :])
                if again:
                    sp.wait_ge(sem("y_ok"), t - NB4 + 1)
                move(f"x1_in{k}", f_r[k][2][0:n, :], x1_d[r, :])

            for k in range(NB4):
                out_tile(k, k, 0)
            with sp.Fori(0, NPT // NB4 - 1) as i:
                for k in range(NB4):
                    out_tile(NB4 * i + NB4 + k, k, i + 1)
            out_tile(SAMPLE, 0, NPT // NB4)
            sp.wait_ge(sem("y_out0"), 16 * (NPT // NB4 + 1))
            for k in range(1, NB4):
                sp.wait_ge(sem(f"y_out{k}"), 16 * (NPT // NB4))
            sp.wait_ge(sem("kv_out"), 16 * 4)
            sp.wait_ge(sem("win_out"), 16 * 4)
            sp.wait_ge(sem("state_out"), 16 * 6)
            sp.wait_ge(sem("st_done"), 32 * NT)

        @block.gpsimd
        def _(pool):
            st = Steps(pool, sem("pool_step"))

            def rotate(t, p):
                pool.wait_ge(sem("rope_in"), 16 * (t + 1))
                pool.wait_ge(sem("c_q"), t + 1)
                pool.wait_ge(sem("c_kv"), t + 1)
                qk = qkv[:, 0:10, :]
                cos = rope_t[:, 0:ROT].rearrange("p (a c) -> p a c", a=1).broadcast_to([P, 10, ROT])
                msin = rope_t[:, ROT:ROT + 8].rearrange("p (a c) -> p a c", a=1).broadcast_to([P, 10, 8])
                sin = rope_t[:, ROT + 8:2 * ROT].rearrange("p (a c) -> p a c", a=1).broadcast_to([P, 10, 8])
                pool.tensor_tensor(rt[:, 0, :, :], qk[:, :, 0:ROT], cos, ALU.mult)
                pool.tensor_tensor(rt[:, 1, :, 0:8], qk[:, :, 8:16], msin, ALU.mult)
                st(pool.tensor_tensor(rt[:, 1, :, 8:16], qk[:, :, 0:8], sin, ALU.mult))
                pool.tensor_tensor(qk[:, :, 0:ROT], rt[:, 0, :, :], rt[:, 1, :, :], ALU.add).then_inc(sem("rope_ok"), 1)
                if past(t):
                    pool.wait_ge(sem("g_pv1"), t)
                apart(pool)
                pool.tensor_copy(vk[p][:], qkv[:, 10:12, :]).then_inc(sem("vk_ok"), 1)

            def scatter(t, p):
                if past(32 * t):
                    pool.wait_ge(sem("scat"), 32 * t)
                apart(pool)
                pool.wait_ge(sem("dst_ok"), t + 1)
                st(pool.tensor_copy(tok_s[:, 0:1], tokid[:, one(t)]))
                apart(pool)
                st(pool.tensor_scalar(tok_s[:, 1:2], tok_s[:, 0:1], float(NT * P), 0.0, ALU.add, ALU.add))
                apart(pool)
                for k in range(2):
                    pool.indirect_dma_start(list_d, bass.IndirectOffsetOnAxis(ap=dst[:, k:k + 1], axis=0),
                                            tok_s[:, k:k + 1], None).then_inc(sem("scat"), 16)

            pool.wait_ge(sem("const_in"), 16 * 26)
            def turn(t, p):
                if has(t - 2):
                    scatter(t - 2, p)
                if has(t):
                    rotate(t, p)

            walk(pool, turn, st, STEPS["pool"])

            st(pool.tensor_copy(sidx_n[:], sidx_f[:]))
            pool.wait_ge(sem("ye"), 1)
            pool.indirect_dma_start(rows_d, bass.IndirectOffsetOnAxis(ap=sidx_n[:], axis=0), yrow[:], None).then_inc(sem("row_st"), 16)
            pool.wait_ge(sem("idx_ok"), 1)
            pool.wait_ge(sem("cnt_ok"), 1)
            pool.wait_ge(sem("st_done"), 32 * NT)
            with pool.Fori(0, NE) as e:
                n = pool.value_load(cnt_i[0:1, 0, bass.ds(e, 1)], min_val=1, max_val=CAP)
                g0 = pool.value_load(cnt_i[0:1, 1, bass.ds(e, 1)], min_val=0, max_val=NB)
                with pool.Fori(0, n) as b:
                    pool.wait_ge(sem("g_x"), g0 + b + 1)
                    apart(pool)
                    pool.tensor_copy(idx[:], idx_all[:, bass.ds(e * CAP + b, 1)]).then_inc(sem("idx1"), 1)
                    pool.wait_ge(sem("idx1"), g0 + b + 1)
                    apart(pool)
                    pool.indirect_dma_start(xg[:], None, h2_d, bass.IndirectOffsetOnAxis(ap=idx[:], axis=0)).then_inc(sem("gath"), 16)
                    pool.wait_ge(sem("row_st"), 16 * (g0 + b + 1))
                    apart(pool)
                    pool.tensor_copy(sidx[:], sidx_n[:]).then_inc(sem("sidx1"), 1)
                    pool.wait_ge(sem("sidx1"), 2 * (g0 + b) + 1)
                    apart(pool)
                    pool.tensor_copy(sidx_n[:], sidx_all[:, bass.ds(e * CAP + b, 1)]).then_inc(sem("sidx1"), 1)
                    pool.wait_ge(sem("ye"), g0 + b + 1)
                    pool.wait_ge(sem("sidx1"), 2 * (g0 + b) + 2)
                    apart(pool)
                    pool.indirect_dma_start(rows_d, bass.IndirectOffsetOnAxis(ap=sidx[:], axis=0), yrow[:], None).then_inc(sem("row_st"), 16)

            blocks = pool.value_load(cnt_i[0:1, 2, 0:1], min_val=0, max_val=NB)
            pool.wait_ge(sem("g_x"), blocks + 1)
            apart(pool)
            pool.indirect_dma_start(xg[:], None, h2_d, bass.IndirectOffsetOnAxis(ap=idx[:], axis=0)).then_inc(sem("gath"), 16)
            pool.wait_ge(sem("row_st"), 16 * blocks + 16)
            apart(pool)
            st(pool.tensor_copy(sidx[:], sidx_n[:]))
            pool.wait_ge(sem("ye"), blocks + 1)
            apart(pool)
            pool.indirect_dma_start(rows_d, bass.IndirectOffsetOnAxis(ap=sidx[:], axis=0), yrow[:], None).then_inc(sem("row_st"), 16)

        @block.scalar
        def _(act):
            st = Steps(act, sem("act_step"))
            A = nc.scalar.activation
            copy = ACT.Copy

            act.preload_act_table_set("natural_log_exp_and_others")
            act.wait_ge(sem("c_in"), 16)
            A(cs[:], cc[:], ACT.Exp, scale=-1.0).then_inc(sem("c_exp"), 1)

            def move(name, to, frm):
                act.dma_start(to, frm).then_inc(sem(name), 16)

            for s_ in range(2):
                move("small_in", mT[s_:s_ + 1, :, :].rearrange("p a b -> p (a b)"), row(a["g_mix"]))
                move("small_in", hT[s_:s_ + 1, :, :].rearrange("p a b -> p (a b)"), row(a["g_ffn"]))
            for j, buf in enumerate((yf, smf, xr, mix, row_gate, row_g2)):
                move("small_in", buf[0:2, :], row(a["b_ada"][j * D:(j + 1) * D]).broadcast_to([2, D]))
            for to, name in ((ident[:], "c_ident"), (cmask[:], "c_cmask"), (lower[:], "c_lower"),
                             (amask[:], "c_amask"), (iotas[:], "c_iotas"), (tokid[:], "c_tokid"),
                             (padcol[:], "c_padcol"), (taps[:], "taps")):
                move("const_in", to, a[name])
            move("const_in", sidx_f[:], a["c_trash"][0, :].rearrange("(n a) -> n a", a=1))
            move("const_in", w_r[:], a["w_r"].rearrange("(p k) n -> p k n", k=KT))
            move("const_in", b_r[:], row(a["b_r"]).broadcast_to([P, NG + NE]))
            move("const_in", g_mh[:, :, :].rearrange("p a b -> p (a b)"), row(a["g_mh"]).broadcast_to([P, MH * MD]))
            move("const_in", sinks[:], row(a["sinks"]).broadcast_to([P, NH]))
            move("const_in", b_i[:], a["b_ig"].rearrange("(n a) -> n a", a=1))
            move("const_in", b_f[:], a["b_fg"].rearrange("(n a) -> n a", a=1))
            move("const_in", kw[:], a["state_C"].rearrange("h v k -> v h k"))
            move("const_in", C_s[:, :, MD], a["state_n"].rearrange("h k -> k h"))
            move("const_in", m_sa[:], a["state_m"].rearrange("(n a) -> n a", a=1))
            move("const_in", qT[:, 0, :], a["cache_k"])
            move("const_in", vs[:].rearrange("p a b -> p (a b)"), a["cache_v"])
            move("const_in", hist_in[:], a["state_conv"])
            for j in range(0, NB + 2, P):
                n = min(P, NB + 2 - j)
                move("const_in", list_d[j * P:(j + n) * P, :].rearrange("(b s) a -> b (s a)", s=P), a["c_trash"][0:n, :])

            def norm(t, p):
                act.wait_ge(sem("x_in"), 16 * (t + 1))
                if past(t - 1):
                    act.wait_ge(sem("c_delta"), t - 1)
                if isinstance(t, int) and t - 2 == NPT - 1:
                    act.wait_ge(sem("state_ok"), 1)
                st(A(b56[:], smf, ACT.Square, accum_out=nr[:, 0:1]))
                st(A(nr[:, 1:2], nr[:, 0:1], ACT.Ln, bias=eps_c[:, 0:1], scale=1.0 / D))
                st(A(nr[:, 2:3], nr[:, 1:2], ACT.Exp, scale=-0.5))
                A(smf, smf, copy, scale=nr[:, 2:3]).then_inc(sem("xn_ok"), 1)

            def norm_evac(t, p):
                s_ = 1 if isinstance(t, int) and t == SAMPLE else 0
                act.wait_ge(sem("modc_in"), 16 * 4)
                if past(t):
                    act.wait_ge(sem("g_o"), t)
                act.wait_ge(sem("g_n"), t + 1)
                for k in range(KT):
                    last = A(hT[:, k, :], (b0, b1)[k // 4][:, (k % 4) * P:(k % 4 + 1) * P], ACT.Identity,
                             bias=mixc[:, s_, 1, k:k + 1], scale=mixc[:, s_, 0, k:k + 1])
                last.then_inc(sem("c_n"), 1)

            def evac_q(t, p):
                act.wait_ge(sem("g_q"), t + 1)
                if past(t):
                    act.wait_ge(sem("g_tk"), t)
                if past(t):
                    act.wait_ge(sem("vk_ok"), t)
                if isinstance(t, int) and t == SAMPLE:
                    act.wait_ge(sem("kv_out"), 32)
                A(qkv[:, 0:8, :].rearrange("p a b -> p (a b)"), b2[:], copy).then_inc(sem("c_q"), 1)

            def evac_kv(t, p):
                act.wait_ge(sem("g_kv"), t + 1)
                A(qkv[:, 8:12, :].rearrange("p a b -> p (a b)"), b0[:, 0:256], copy).then_inc(sem("c_kv"), 1)

            def evac_c(i, bank):
                def f(t, p):
                    act.wait_ge(sem(f"g_qk{i}"), t + 1)
                    if past(t):
                        act.wait_ge(sem("conv_ok"), t)
                    A(cT[:, 4 * i:4 * i + 4, CW - 1:], bank[:].rearrange("p (a b) -> p a b", a=4), copy)\
                        .then_inc(sem(f"c_qk{i}"), 1)
                return f

            def evac_vm(t, p):
                act.wait_ge(sem("g_vm"), t + 1)
                if past(t):
                    act.wait_ge(sem("g_delta"), t)
                A(vmo[:, :, 0:MD], b1[:].rearrange("p (a b) -> p a b", a=MH), copy).then_inc(sem("c_vm"), 1)

            def evac_o(t, p):
                act.wait_ge(sem("g_o"), t + 1)
                if past(t):
                    act.wait_ge(sem("mixed_h"), t)
                A(og[:].rearrange("p a b -> p (a b)"), b7[:], ACT.Exp, scale=-1.0).then_inc(sem("c_o"), 1)

            def sig_o(t, p):
                act.wait_ge(sem("o_1e"), t + 1)
                st(A(og[:], og[:], ACT.Ln))
                A(og[:], og[:], ACT.Exp, scale=-1.0).then_inc(sem("o_sig"), 1)

            def prep(t, p):
                act.wait_ge(sem("conv_y"), t + 1)
                if past(t):
                    act.wait_ge(sem("g_pv1"), t)
                A(pTf, yf, ACT.Exp, scale=-1.0).then_inc(sem("silu_e"), 1)
                act.wait_ge(sem("silu_1e"), t + 1)
                st(A(pTf, pTf, ACT.Ln))
                A(pTf, pTf, ACT.Exp, scale=-1.0).then_inc(sem("silu_s"), 1)

            def gate(t, p):
                act.wait_ge(sem("f_neg"), t + 1)
                st(A(gr[:, 2, :], gr[:, 2, :], ACT.Exp))
                A(gr[:, 2, :], gr[:, 2, :], ACT.Ln, bias=one_c[0:MH, 0:1]).then_inc(sem("f_log"), 1)
                m_in = m_sa if isinstance(t, int) and t == SAMPLE else m_st[1 - p]
                act.wait_ge(sem("gate_m"), t + 1)
                A(stk[32:32 + MH, :], stk[0:MH, :], ACT.Exp, bias=g1c[:, 0:1])
                A(stk[64:64 + MH, :], gr[:, 4, :], ACT.Exp, bias=m_in[:, 0:1], scale=-1.0)
                A(stk[96:96 + MH, :], gr[:, 5, :], ACT.Exp, scale=-1.0)
                A(g1c[:, 1:2], gr[:, 4, P - 1:P], ACT.Exp, bias=m_in[:, 0:1], scale=-1.0).then_inc(sem("gate_e"), 1)

            def kr(t, p):
                act.wait_ge(sem("g_kr"), t + 1)
                act.wait_ge(sem("c_cols"), t + 1)
                if isinstance(t, int) and t == SAMPLE:
                    act.wait_ge(sem("state_out"), 48)
                for h in range(MH):
                    last = A(kw[:, h, :], b56[:, h * MD:(h + 1) * MD], copy, scale=cols[:, 32 + h:33 + h])
                last.then_inc(sem("c_kw"), 1)

            def probs(j):
                def f(t, p):
                    act.wait_ge(sem(f"smax{j}"), t + 1)
                    for g in range(G):
                        A(sm[:, g, :], sm[:, g, :], ACT.Exp, bias=at4[:, 1, g:g + 1], scale=HD ** -0.5,
                          accum_out=at4[:, 2, g:g + 1])
                    A(at4[:, 3, :], at4[:, 3, :], ACT.Exp).then_inc(sem(f"probs{j}"), 1)
                return f

            def w_exp(t, p):
                act.wait_ge(sem("w_arg"), t + 1)
                for h in range(MH):
                    last = A(wT[:, h, :], wT[:, h, :], ACT.Exp, bias=cols[:, h:h + 1])
                last.then_inc(sem("w_exp"), 1)

            def probs_t(j):
                def f(t, p):
                    act.wait_ge(sem(f"g_pt{j}"), t + 1)
                    A(pT[:, 1, :, :], b34[:, 512:1024].rearrange("p (a b) -> p a b", a=4), copy).then_inc(sem(f"c_pta{j}"), 1)
                return f

            def inter(t, p):
                act.wait_ge(sem("g_inter"), t + 1)
                act.wait_ge(sem("g_negm"), t + 1)
                for h in range(MH):
                    last = A(num[:, h, :], head2(b34, h), copy, scale=cols[:, 64 + h:65 + h])
                last.then_inc(sem("c_inter"), 1)

            def mid(t, p):
                act.wait_ge(sem("c_num"), t + 1)
                act.wait_ge(sem("g_intra"), t + 1)
                for h in range(MH):
                    last = A(wT[:, h, :], num[:, h, 0:MD], ACT.Square, accum_out=ml4[:, 2, h:h + 1])
                last.then_inc(sem("h_sq"), 1)
                act.wait_ge(sem("h_ms"), t + 1)
                st(A(ml4[:, 4, :], ml4[:, 3, :], ACT.Ln, bias=eps_c[:, 0:1], scale=1.0 / MD))
                A(ml4[:, 5, :], ml4[:, 4, :], ACT.Exp, scale=-0.5).then_inc(sem("h_rs"), 1)

            def mixT(t, p):
                act.wait_ge(sem("g_mx0"), t + 1)
                A(mT[:, 0:4, :], b2[:].rearrange("p (a b) -> p a b", a=4), copy)
                act.wait_ge(sem("g_mx1"), t + 1)
                A(mT[:, 4:8, :], b0[:].rearrange("p (a b) -> p a b", a=4), copy).then_inc(sem("c_mx"), 1)

            def proj(t, p):
                act.wait_ge(sem("x1_ok"), t + 1)
                act.wait_ge(sem("c_delta"), t + 1)
                if isinstance(t, int) and t in (NPT - 1, SAMPLE):
                    act.wait_ge(sem("state_ok"), 1 + (t == SAMPLE))
                st(A(b56[:], xr[:], ACT.Square, accum_out=nr[:, 4:5]))
                st(A(nr[:, 5:6], nr[:, 4:5], ACT.Ln, bias=eps_c[:, 0:1], scale=1.0 / D))
                A(nr[:, 6:7], nr[:, 5:6], ACT.Exp, scale=-0.5).then_inc(sem("rstd2"), 1)

            def route_hT(t, p):
                for i, bank in ((0, b0), (1, b1)):
                    act.wait_ge(sem(f"g_hT{i}"), t + 1)
                    A(mT[:, 4 * i:4 * i + 4, :], bank[:].rearrange("p (a b) -> p a b", a=4), copy).then_inc(sem(f"c_hT{i}"), 1)

            def route(t, p):
                act.wait_ge(sem("g_max"), t + 1)
                A(rc[:, 4:8], lg8[:, 0:NG], ACT.Exp, bias=rc[:, 0:1], accum_out=rc[:, 1:2]).then_inc(sem("g_exp"), 1)
                act.wait_ge(sem("e_dif"), t + 1)
                A(rc[:, 10:11], rc[:, 9:10], ACT.Exp).then_inc(sem("e_exp"), 1)

            act.wait_ge(sem("const_in"), 16 * 26)
            act.wait_ge(sem("init_ok"), 1)
            def turn(t, p):
                if has(t - 1):
                    kr(t - 1, 1 - p)
                    w_exp(t - 1, 1 - p)
                    probs(0)(t - 1, 1 - p)
                if has(t):
                    evac_q(t, p)
                if has(t - 1):
                    probs_t(0)(t - 1, 1 - p)
                if has(t):
                    evac_kv(t, p)
                if has(t - 1):
                    inter(t - 1, 1 - p)
                    probs(1)(t - 1, 1 - p)
                    mid(t - 1, 1 - p)
                if has(t):
                    evac_c(0, b1)(t, p)
                if has(t - 1):
                    probs_t(1)(t - 1, 1 - p)
                if has(t):
                    evac_c(1, b2)(t, p)
                    evac_vm(t, p)
                if has(t - 1):
                    mixT(t - 1, 1 - p)
                if has(t + 1):
                    norm(t + 1, 1 - p)
                if has(t):
                    prep(t, p)
                    gate(t, p)
                if has(t - 1):
                    proj(t - 1, 1 - p)
                    route_hT(t - 1, 1 - p)
                if has(t):
                    evac_o(t, p)
                if has(t + 1):
                    norm_evac(t + 1, 1 - p)
                if has(t - 1):
                    route(t - 1, 1 - p)
                if has(t):
                    sig_o(t, p)

            norm(0, 0)
            norm_evac(0, 0)
            walk(act, turn, st, STEPS["act"])

            act.preload_act_table_set("silu_and_others")
            act.wait_ge(sem("cnt_ok"), 1)
            with act.Fori(0, NE) as e:
                n = act.value_load(cnt_i[0:1, 0, bass.ds(e, 1)], min_val=1, max_val=CAP)
                g0 = act.value_load(cnt_i[0:1, 1, bass.ds(e, 1)], min_val=0, max_val=NB)
                with act.Fori(0, n) as b:
                    act.wait_ge(sem("gu"), 2 * (g0 + b) + 1)
                    A(e_a[:], b2[:], ACT.Silu).then_inc(sem("ge"), 1)
                    act.wait_ge(sem("g_aT"), 2 * (g0 + b) + 1)
                    A(aT[:, 0:2, :], b34[:, 0:256].rearrange("p (a b) -> p a b", a=2), copy).then_inc(sem("c_a0"), 1)
                    act.wait_ge(sem("dn"), g0 + b + 1)
                    act.wait_ge(sem("row_st"), 16 * (g0 + b + 2))
                    A(yrow[:], b56[:], copy).then_inc(sem("ye"), 1)

            act.preload_act_table_set("natural_log_exp_and_others")

            def first_row(t, k, turn, n=P):
                act.wait_ge(sem(f"x1_in{k}"), 48 * (turn + 1))
                st(A(f_g[k][:], gate_all[:, :, one(t)].rearrange("p a b -> p (a b)"), copy))
                A(f_r[k][0][0:n, :], f_r[k][0][0:n, :], copy, scale=f_g[k][0:n, 0:1]).then_inc(sem("f_r0"), 1)

            def last_norm(t, k, turn, n=P):
                act.wait_ge(sem("f_x"), t + 1)
                if not (isinstance(turn, int) and turn == 0):
                    act.wait_ge(sem(f"y_out{k}"), 16 * turn)
                st(A(f_r[k][3][0:n, :], f_r[k][2][0:n, :], ACT.Square, accum_out=nr[0:n, 0:1]))
                st(A(nr[0:n, 1:2], nr[0:n, 0:1], ACT.Ln, bias=eps_c[0:n, 0:1], scale=1.0 / D))
                A(nr[0:n, k + 2:k + 3], nr[0:n, 1:2], ACT.Exp, scale=-0.5).then_inc(sem("f_rs"), 1)

            def y_store(t, k):
                act.wait_ge(sem("y_ok"), t + 1)
                to, n = (o["y_s"], DEC) if isinstance(t, int) and t == SAMPLE else (o["y_p"][rows(t), :], P)
                act.dma_start(to, f_r[k][3][0:n, :]).then_inc(sem(f"y_out{k}"), 16)

            def last_tiles(t, turn):
                for k in range(NB4):
                    nxt = t + k + 1
                    sample = isinstance(nxt, int) and nxt == SAMPLE
                    first_row(nxt, (k + 1) % NB4, turn + (k + 1) // NB4, DEC if sample else P)
                    last_norm(t + k, k, turn)
                    if k or not (isinstance(t, int) and t == 0):
                        y_store(t + k - 1, (k - 1) % NB4)

            first_row(0, 0, 0)
            start = st.n
            last_tiles(0, 0)
            with act.Fori(1, NPT // NB4 - 1) as i:
                st.base, st.n = 3 * NB4 * (i - 1), start + 3 * NB4
                last_tiles(NB4 * i, i)
            st.base, st.n = 0, start + 3 * (NPT - NB4)
            last_tiles(NPT - NB4, NPT // NB4 - 1)
            last_norm(SAMPLE, 0, NPT // NB4, DEC)
            y_store(SAMPLE - 1, NB4 - 1)
            y_store(SAMPLE, 0)

        @block.tensor
        def _(pe):
            mm = nc.tensor.matmul

            def tr(out, in_, n=P):
                return nc.tensor.transpose(out, in_, ident[0:n, 0:n])

            pe.wait_ge(sem("c_silu"), 1)
            for i in range(NADA):
                pe.wait_ge(sem(f"ada_in{i % 2}"), 16 * (i // 2 + 1))
                if past(i - 1):
                    pe.wait_ge(sem("ada_row"), i - 1)
                for k in range(KT):
                    last = mm((b0, b1)[i % 2][0:2, :], cs[:, k, :], ada[i % 2][:, k, :], start=k == 0, stop=k == KT - 1)
                last.then_inc(sem("ada_mm"), 1)
            pe.wait_ge(sem("const_in"), 16 * 26)
            for h in range(MH):
                last = tr(b34[:, h * P:(h + 1) * P], kw[:, h, :])
            tr(b34[:, 512:640], qT[:, 0, :]).then_inc(sem("g_state"), 1)

            def norm(t, p):
                pe.wait_ge(sem("xn_ok"), t + 1)
                if past(t):
                    pe.wait_ge(sem("c_gates"), t)
                if past(t - 1):
                    pe.wait_ge(sem("c_hT0"), t - 1)
                if isinstance(t, int) and t == 0:
                    pe.wait_ge(sem("ada_row"), NADA)
                for k in range(4):
                    last = tr(b0[:, k * P:(k + 1) * P], smf[:, k:D:KT])
                if past(t):
                    pe.wait_ge(sem("c_vm"), t)
                if past(t - 1):
                    pe.wait_ge(sem("c_hT1"), t - 1)
                for k in range(4):
                    last = tr(b1[:, k * P:(k + 1) * P], smf[:, 4 + k:D:KT])
                last.then_inc(sem("g_n"), 1)

            def rowgroup(name, bank, c0, n, free, back):
                def f(t, p):
                    pe.wait_ge(sem("c_n"), t + 1)
                    if past(t + 1 - back):
                        pe.wait_ge(sem(free), t + 1 - back)
                    for k in range(KT):
                        last = mm(bank[:, 0:n], hT[:, k, :], w_in[:, k, c0:c0 + n], start=k == 0, stop=k == KT - 1)
                    last.then_inc(sem(name), 1)
                return f

            def colgroup(i, bank, free):
                def f(t, p):
                    pe.wait_ge(sem(free), t + 1)
                    for c in range(4):
                        for k in range(KT):
                            at = C0 + (4 * i + c) * P
                            last = mm(bank[:, c * P:(c + 1) * P], w_in[:, k, at:at + P], hT[:, k, :],
                                      start=k == 0, stop=k == KT - 1)
                    last.then_inc(sem(f"g_qk{i}"), 1)
                return f

            def gates(t, p):
                pe.wait_ge(sem("c_kv"), t + 1)
                for k in range(KT):
                    last = mm(b0[0:32 + MH, 0:P], w_in[:, k, I0:F0 + MH], hT[:, k, :], start=k == 0, stop=k == KT - 1)
                last.then_inc(sem("g_gates"), 1)

            def qk(t, p):
                pe.wait_ge(sem("rope_ok"), t + 1)
                if past(t):
                    pe.wait_ge(sem("c_ptd1"), t)
                if past(t):
                    pe.wait_ge(sem("c_pta1"), t)
                if isinstance(t, int) and t == 0:
                    pe.wait_ge(sem("c_state"), 1)
                for g in range(G):
                    tr(b34[:, g * P:(g + 1) * P], qkv[:, 2 * g:2 * g + 2, :].rearrange("p a b -> p (a b)"))
                tr(b34[:, 512:640], qkv[:, 8:10, :].rearrange("p a b -> p (a b)")).then_inc(sem("g_tk"), 1)

            def gate(t, p):
                pe.wait_ge(sem("diag_ok"), t + 1)
                pe.wait_ge(sem("c_o"), t + 1)
                mm(b7[:], negones[:], md, start=True, stop=True).then_inc(sem("g_negm"), 1)
                pe.wait_ge(sem("stk_ok"), t + 1)
                pe.wait_ge(sem("c_tk"), t + 1)
                tr(b34[:, 640:768], stk[:])
                mm(b34[:, 768:768 + MH], ones[0:MH, :], dd[:], start=True, stop=True).then_inc(sem("g_cols"), 1)

            def kr(t, p):
                pe.wait_ge(sem("silu_y"), t + 1)
                pe.wait_ge(sem("xn_ok"), upto(t + 2))
                if past(t):
                    pe.wait_ge(sem("rstd2"), t)
                if isinstance(t, int) and t == SAMPLE:
                    pe.wait_ge(sem("state_ok"), 1)
                for h in range(MH):
                    last = tr(b56[:, h * P:(h + 1) * P], y[:, MH + h, :])
                last.then_inc(sem("g_kr"), 1)
                for h in range(MH):
                    last = mm(b56[:, 512 + h * P:512 + (h + 1) * P], y[:, MH + h, :], y[:, h, :], start=True, stop=True)
                last.then_inc(sem("g_sc"), 1)

            def scores(j):
                def f(t, p):
                    if j == 0:
                        pe.wait_ge(sem("c_cols"), t + 1)
                    else:
                        pe.wait_ge(sem("c_inter"), t + 1)
                    kp = prev(t, p, kT, kTs)
                    r = slice(HD * j, HD * j + HD)
                    for g in range(G):
                        mm(b34[:, g * 256:g * 256 + P], qT[r, g, :], kp[r, :], start=True, stop=True)
                        last = mm(b34[:, g * 256 + P:g * 256 + 256], qT[r, g, :], kT[p][r, :], start=True, stop=True)
                    last.then_inc(sem(f"g_s{j}"), 1)
                return f

            def intra(t, p):
                pe.wait_ge(sem("c_T"), t + 1)
                pe.wait_ge(sem("c_kw"), t + 1)
                for h in range(MH):
                    last = mm(head2(b56, h), wT[:, h, :], vmo[:, h, :], start=True, stop=True)
                last.then_inc(sem("g_intra"), 1)

            def turned(j):
                def f(t, p):
                    pe.wait_ge(sem(f"probs{j}"), t + 1)
                    for half in range(2):
                        for g in range(G):
                            last = tr(b34[:, half * 512 + g * P:half * 512 + (g + 1) * P], sm[:, g, half * P:(half + 1) * P])
                    last.then_inc(sem(f"g_pt{j}"), 1)
                return f

            def pv(j):
                def f(t, p):
                    pe.wait_ge(sem(f"c_ptd{j}"), t + 1)
                    pe.wait_ge(sem(f"c_pta{j}"), t + 1)
                    pe.wait_ge(sem("vk_ok"), t + 1)
                    vp = prev(t, p, vk, vs)
                    for g in range(G):
                        at = j * 256 + g * HD
                        mm(b7[:, at:at + HD], pT[:, 0, g, :], vp[:, j, :], start=True, stop=False)
                        last = mm(b7[:, at:at + HD], pT[:, 1, g, :], vk[p][:, j, :], start=False, stop=True)
                    last.then_inc(sem(f"g_pv{j}"), 1)
                return f

            def inter(t, p):
                C = C_s if isinstance(t, int) and t == SAMPLE else C_p
                if past(t):
                    pe.wait_ge(sem("c_delta"), t)
                pe.wait_ge(sem("c_ptd0"), t + 1)
                pe.wait_ge(sem("c_pta0"), t + 1)
                for h in range(MH):
                    last = mm(head2(b34, h), y[:, h, :], C[:, h, :], start=True, stop=True)
                last.then_inc(sem("g_inter"), 1)

            def delta(t, p):
                C = C_s if isinstance(t, int) and t == SAMPLE else C_p
                pe.wait_ge(sem("c_num"), t + 1)
                for h in range(MH):
                    last = mm(head2(b56, h), kw[:, h, :], vmo[:, h, :], start=True, stop=True)
                last.then_inc(sem("g_delta"), 1)
                if isinstance(t, int) and t in (NPT - 1, SAMPLE):
                    pe.wait_ge(sem("c_delta"), t + 1)
                    for h in range(MH):
                        last = tr(b56[:, h * P:(h + 1) * P], C[:, h, 0:MD])
                    last.then_inc(sem("g_stout"), 1)

            def mixT(t, p):
                pe.wait_ge(sem("mixed_h"), t + 1)
                pe.wait_ge(sem("att1"), t + 1)
                pe.wait_ge(sem("c_qk1"), upto(t + 2))
                for k in range(4):
                    last = tr(b2[:, k * P:(k + 1) * P], mix[:, k:D:KT])
                last.then_inc(sem("g_mx0"), 1)
                pe.wait_ge(sem("c_gates"), upto(t + 2))
                for k in range(4):
                    last = tr(b0[:, k * P:(k + 1) * P], mix[:, 4 + k:D:KT])
                last.then_inc(sem("g_mx1"), 1)

            def proj(t, p):
                if isinstance(t, int) and t == 0:
                    pe.wait_ge(sem("wout_in"), 16)
                pe.wait_ge(sem("c_mx"), t + 1)
                pe.wait_ge(sem("c_vm"), upto(t + 2))
                for i, bank in ((0, b1), (1, b2)):
                    for k in range(KT):
                        last = mm(bank[:], mT[:, k, :], w_out[:, k, i * 512:(i + 1) * 512], start=k == 0, stop=k == KT - 1)
                    last.then_inc(sem(f"g_pr{i}"), 1)

            def route(t, p):
                pe.wait_ge(sem("h2"), t + 1)
                for i, bank in ((0, b0), (1, b1)):
                    for k in range(4):
                        last = tr(bank[:, k * P:(k + 1) * P], mix[:, 4 * i + k:D:KT])
                    last.then_inc(sem(f"g_hT{i}"), 1)
                pe.wait_ge(sem("c_hT1"), t + 1)
                for k in range(KT):
                    last = mm(b2[:, 0:NG + NE], mT[:, k, :], w_r[:, k, :], start=k == 0, stop=k == KT - 1)
                last.then_inc(sem("g_lg"), 1)

            def rank(t, p):
                pe.wait_ge(sem("M_ok"), t + 1)
                mm(b2[:, 64:64 + NE], lower[:], oh[:, 2, :], start=True, stop=False)
                mm(b2[:, 64:64 + NE], ones[:], Msum[:], start=False, stop=True).then_inc(sem("g_rank"), 1)

            pe.wait_ge(sem("win_in"), 16 * KT)
            def turn(t, p):
                if has(t - 1):
                    qk(t - 1, 1 - p)
                    gate(t - 1, 1 - p)
                if has(t - 2):
                    rank(t - 2, p)
                if has(t - 1):
                    kr(t - 1, 1 - p)
                    scores(0)(t - 1, 1 - p)
                if has(t):
                    rowgroup("g_q", b2, Q0, 512, "c_rank", 2)(t, p)
                if has(t - 1):
                    intra(t - 1, 1 - p)
                    turned(0)(t - 1, 1 - p)
                if has(t):
                    rowgroup("g_kv", b0, K0, 256, "c_n", 0)(t, p)
                if has(t - 1):
                    pv(0)(t - 1, 1 - p)
                    inter(t - 1, 1 - p)
                if has(t):
                    gates(t, p)
                if has(t - 1):
                    scores(1)(t - 1, 1 - p)
                    delta(t - 1, 1 - p)
                if has(t):
                    colgroup(0, b1, "c_n")(t, p)
                if has(t - 1):
                    turned(1)(t - 1, 1 - p)
                if has(t):
                    colgroup(1, b2, "c_q")(t, p)
                if has(t - 1):
                    pv(1)(t - 1, 1 - p)
                if has(t):
                    rowgroup("g_vm", b1, VM0, 512, "c_qk0", 0)(t, p)
                if has(t - 1):
                    mixT(t - 1, 1 - p)
                    proj(t - 1, 1 - p)
                if has(t):
                    rowgroup("g_o", b7, O0, 512, "att1", 1)(t, p)
                if has(t - 1):
                    route(t - 1, 1 - p)
                if has(t + 1):
                    norm(t + 1, 1 - p)

            norm(0, 0)
            walk(pe, turn)

            pe.wait_ge(sem("c_rank"), NT)
            mm(b2[:, 0:NE], ones[:], Msum[:], start=True, stop=True).then_inc(sem("g_cnt"), 1)
            pe.wait_ge(sem("lists_in"), 16 * 5)
            for j in range(5):
                n = min(P, NB - j * P)
                last = tr(b34[:, j * P:j * P + n], lists[0:n, j, :], n)
                if j == 0:
                    last.then_inc(sem("g_x"), 1)
            last.then_inc(sem("g_lists"), 1)
            pe.wait_ge(sem("cnt_ok"), 1)
            pe.wait_ge(sem("idx_ok"), 1)

            def rows_in(g, q):
                pe.wait_ge(sem("gath"), 16 * (g + 1))
                for c in range(4):
                    last = tr((b0, b1)[q][:, c * P:(c + 1) * P], xg[:, 4 * q + c:D:KT])
                if q == 1:
                    last.then_inc(sem("g_x"), 1)

            def expert(e, k, i):
                w_g, w_u = ([half for piece in we[k][q] for half in (piece[:, 0:FE], piece[:, FE:D])] for q in range(2))
                w_d = we[k][2]
                n = pe.value_load(cnt_i[0:1, 0, bass.ds(e, 1)], min_val=1, max_val=CAP)
                g0 = pe.value_load(cnt_i[0:1, 1, bass.ds(e, 1)], min_val=0, max_val=NB)
                pe.wait_ge(sem(f"we_in{k}"), WE_IN[k] * (i + 1))
                apart(pe)
                with pe.Fori(0, n) as b:
                    g = g0 + b
                    pe.wait_ge(sem("c_x"), g + 1)
                    for wt, bank in ((w_g, b2), (w_u, b7)):
                        for c in range(KT):
                            last = mm(bank[:], xT[:, c, :], wt[c], start=c == 0, stop=c == KT - 1)
                        last.then_inc(sem("gu"), 1)
                    rows_in(g + 1, 0)
                    for half in range(2):
                        pe.wait_ge(sem("a_ok"), 2 * g + 1 + half)
                        for j in range(2):
                            at = 2 * half + j
                            last = tr(b34[:, half * 512 + j * P:half * 512 + (j + 1) * P], e_a[:, at * P:(at + 1) * P])
                        last.then_inc(sem("g_aT"), 1)
                    rows_in(g + 1, 1)
                    pe.wait_ge(sem("ye"), g + 1)
                    for j in range(FT):
                        if j % 2 == 0:
                            pe.wait_ge(sem(f"c_a{j // 2}"), g + 1)
                        for q in range(2):
                            last = mm(b56[:, q * 512:(q + 1) * 512], aT[:, j, :], w_d[j][:, q * 512:(q + 1) * 512],
                                      start=j == 0, stop=j == FT - 1)
                    last.then_inc(sem("dn"), 1)

            rows_in(0, 0)
            rows_in(0, 1)
            with pe.Fori(0, NE // 3) as i:
                for k in range(3):
                    expert(3 * i + k, k, i)
            for k in range(NE % 3):
                expert(NE // 3 * 3 + k, k, NE // 3)

        @block.vector
        def _(dve):
            st = Steps(dve, sem("dve_step"))
            v = nc.vector

            def bc(ap, shape):
                return ap.rearrange("p (a c) -> p a c", c=1).broadcast_to(shape)

            v.memset(cT[:], 0.0)
            v.memset(stk[:], 0.0)
            v.memset(Msum[:], 0.0)
            v.memset(C_p[:], 0.0)
            v.memset(m_st[1][:], 0.0)
            v.memset(lg8[:], -3e38)
            v.memset(vmo[:, :, MD:MD + 1], 1.0)
            v.memset(ones[:], 1.0)
            v.memset(negones[:], -1.0)
            v.memset(one_c[:], 1.0)
            v.memset(eps_c[:], EPS).then_inc(sem("init_ok"), 1)
            dve.wait_ge(sem("c_exp"), 1)
            st(v.tensor_scalar(cs[:], cs[:], 1.0, None, ALU.add))
            st(v.reciprocal(cs[:], cs[:]))
            v.tensor_tensor(cs[:], cc[:], cs[:], ALU.mult).then_inc(sem("c_silu"), 1)
            dve.wait_ge(sem("small_in"), 16 * (4 + NADA // 2))
            gm, gf = (z[:, :, :].rearrange("p a b -> p (a b)") for z in (mT, hT))
            for i in range(NADA):
                buf = (yf, smf, xr, mix, row_gate, row_g2)[i // 2]
                r = buf[0:2, (i % 2) * 512:(i % 2) * 512 + 512]
                dve.wait_ge(sem("ada_mm"), i + 1)
                out = v.tensor_tensor(r, (b0, b1)[i % 2][0:2, :], r, ALU.add)
                if i // 2 in (1, 4):
                    st(out)
                    g_ = (gm if i // 2 == 1 else gf)[0:2, (i % 2) * 512:(i % 2) * 512 + 512]
                    out = v.scalar_tensor_tensor(out=r, in0=r, scalar=1.0, in1=g_, op0=ALU.add, op1=ALU.mult)
                out.then_inc(sem("ada_row"), 1)
            dve.wait_ge(sem("g_state"), 1)
            v.tensor_copy(C_s[:, :, 0:MD], b34[:, 0:512].rearrange("p (a b) -> p a b", a=MH))
            v.tensor_copy(kTs[:], b34[:, 512:640]).then_inc(sem("c_state"), 1)
            dve.wait_ge(sem("const_in"), 16 * 26)

            def gates_evac(t, p):
                dve.wait_ge(sem("g_gates"), t + 1)
                v.tensor_scalar(gr[:, 0, :], b0[0:MH, 0:P], b_i[:, 0:1], None, ALU.add)
                v.tensor_scalar(gr[:, 1, :], b0[32:32 + MH, 0:P], b_f[:, 0:1], None, ALU.add).then_inc(sem("c_gates"), 1)

            def qk(t, p):
                dve.wait_ge(sem("g_tk"), t + 1)
                v.tensor_copy(qT[:], b34[:, 0:512].rearrange("p (a b) -> p a b", a=G))
                v.tensor_copy(kT[p][:], b34[:, 512:640]).then_inc(sem("c_tk"), 1)

            def prep(t, p):
                dve.wait_ge(sem("c_qk0"), t + 1)
                dve.wait_ge(sem("c_qk1"), t + 1)
                if past(t):
                    dve.wait_ge(sem("g_inter"), t)
                for c in range(KT):
                    last = v.tensor_scalar(y[:, c, :], cT[:, c, CW - 1:CW - 1 + P], taps[:, CW - 1, c:c + 1],
                                           taps[:, CW, c:c + 1], ALU.mult, ALU.add)
                st(last)
                for j in range(CW - 1):
                    for c in range(KT):
                        last = v.scalar_tensor_tensor(out=y[:, c, :], in0=cT[:, c, j:j + P], scalar=taps[:, j, c:c + 1],
                                                      in1=y[:, c, :], op0=ALU.mult, op1=ALU.add)
                    if j < CW - 2:
                        st(last)
                last.then_inc(sem("conv_y"), 1)
                dve.wait_ge(sem("conv_y"), t + 1)
                if isinstance(t, int) and t >= NPT - 1:
                    at = P if t < NPT else DEC
                    st(v.tensor_copy(hist[t == SAMPLE][:].rearrange("p j c -> p c j"), cT[:, :, at:at + CW - 1]))
                new = hist_in[:].rearrange("p j c -> p c j") if isinstance(t, int) and t == NPT - 1 else cT[:, :, P:P + CW - 1]
                v.tensor_copy(cT[:, :, 0:CW - 1], new).then_inc(sem("conv_ok"), 1)
                dve.wait_ge(sem("silu_e"), t + 1)
                v.tensor_scalar(pTf, pTf, 1e18, 1.0, ALU.min, ALU.add).then_inc(sem("silu_1e"), 1)

            def silu(t, p):
                dve.wait_ge(sem("silu_s"), t + 1)
                v.scalar_tensor_tensor(out=yf[:, 0:512], in0=yf[:, 0:512], scalar=MD ** -0.5, in1=pTf[:, 0:512],
                                       op0=ALU.mult, op1=ALU.mult)
                v.tensor_tensor(yf[:, 512:1024], yf[:, 512:1024], pTf[:, 512:1024], ALU.mult).then_inc(sem("silu_y"), 1)

            def gate(t, p):
                sample = isinstance(t, int) and t == SAMPLE
                m_in = m_sa if sample else m_st[1 - p]
                dve.wait_ge(sem("c_gates"), t + 1)
                if past(t):
                    dve.wait_ge(sem("gate_e"), t)
                v.scalar_tensor_tensor(out=gr[:, 2, :], in0=gr[:, 1, :], scalar=-1.0, in1=gr[:, 1, :],
                                       op0=ALU.mult, op1=ALU.min).then_inc(sem("f_neg"), 1)
                dve.wait_ge(sem("f_log"), t + 1)
                st(v.scalar_tensor_tensor(out=gr[:, 1, :], in0=gr[:, 1, :], scalar=0.0, in1=gr[:, 2, :],
                                          op0=ALU.min, op1=ALU.subtract))
                if sample:
                    v.memset(gr[:, 0, DEC:P], -BIG)
                    st(v.memset(gr[:, 1, DEC:P], 0.0))
                st(v.tensor_tensor_scan(gr[:, 3, :], ones[0:MH, :], gr[:, 1, :], 0.0, ALU.mult, ALU.add))
                if past(t):
                    dve.wait_ge(sem("g_cols"), t)
                st(v.tensor_tensor(stk[0:MH, :], gr[:, 0, :], gr[:, 3, :], ALU.subtract))
                st(v.tensor_tensor_scan(gr[:, 4, :], ones[0:MH, :], stk[0:MH, :], m_in[:, 0:1], ALU.mult, ALU.max))
                st(v.tensor_tensor(gr[:, 5, :], gr[:, 3, :], gr[:, 4, :], ALU.add))
                v.tensor_copy(m_st[p][:], gr[:, 5, P - 1:P])
                v.tensor_scalar(g1c[:, 0:1], gr[:, 4, P - 1:P], -1.0, None, ALU.mult).then_inc(sem("gate_m"), 1)
                if past(t):
                    dve.wait_ge(sem("mixed_h"), t)
                v.tensor_tensor(md, gr[:, 4, :].rearrange("p (a b) -> p a b", a=1).broadcast_to([MH, MH, P]),
                                bc(ident[0:MH, 0:MH], [MH, MH, P]), ALU.mult).then_inc(sem("diag_ok"), 1)
                dve.wait_ge(sem("gate_e"), t + 1)
                v.tensor_scalar(dd[:], ident[0:MH, 0:MH], g1c[:, 1:2], None, ALU.mult).then_inc(sem("stk_ok"), 1)

            def columns(t, p):
                dve.wait_ge(sem("g_cols"), t + 1)
                v.tensor_copy(cols[:], b34[:, 640:768])
                v.tensor_copy(dec[:], b34[:, 768:768 + MH]).then_inc(sem("c_cols"), 1)

            def softmax(j):
                def f(t, p):
                    m = (0 if t == 0 else 2 if t == SAMPLE else 1) if isinstance(t, int) else 1
                    dve.wait_ge(sem(f"g_s{j}"), t + 1)
                    dve.wait_ge(sem("g_pt0" if j else "g_n"), t + 1 if j else upto(t + 2))
                    st(v.tensor_tensor(sm[:], b34[:].rearrange("p (a b) -> p a b", a=4),
                                       amask[:, m:m + 1, :].broadcast_to([P, 4, 2 * P]), ALU.add))
                    st(v.tensor_reduce(at4[:, 0, :], sm[:], AX.X, ALU.max))
                    st(v.scalar_tensor_tensor(out=at4[:, 0, :], in0=at4[:, 0, :], scalar=HD ** -0.5,
                                              in1=sinks[:, 4 * j:4 * j + 4], op0=ALU.mult, op1=ALU.max))
                    v.tensor_scalar(at4[:, 1, :], at4[:, 0, :], -1.0, None, ALU.mult)
                    v.tensor_tensor(at4[:, 3, :], sinks[:, 4 * j:4 * j + 4], at4[:, 0, :], ALU.subtract).then_inc(sem(f"smax{j}"), 1)
                return f

            def weights(t, p):
                dve.wait_ge(sem("g_negm"), t + 1)
                v.tensor_tensor(wT[:], b7[:].rearrange("p (a b) -> p a b", a=MH),
                                cmask[:].rearrange("p (a b) -> p a b", a=1).broadcast_to([P, MH, P]), ALU.add).then_inc(sem("w_arg"), 1)

            def weights2(t, p):
                dve.wait_ge(sem("w_exp"), t + 1)
                dve.wait_ge(sem("g_sc"), t + 1)
                v.tensor_tensor(wT[:], b56[:, 512:1024].rearrange("p (a b) -> p a b", a=MH), wT[:], ALU.mult).then_inc(sem("c_T"), 1)

            def turned(j):
                def f(t, p):
                    dve.wait_ge(sem(f"g_pt{j}"), t + 1)
                    v.tensor_copy(pT[:, 0, :, :], b34[:, 0:512].rearrange("p (a b) -> p a b", a=4)).then_inc(sem(f"c_ptd{j}"), 1)
                return f

            def attend(j):
                def f(t, p):
                    dve.wait_ge(sem(f"probs{j}"), t + 1)
                    st(v.tensor_tensor(at4[:, 4, :], at4[:, 2, :], at4[:, 3, :], ALU.add))
                    st(v.reciprocal(at4[:, 4, :], at4[:, 4, :]))
                    dve.wait_ge(sem(f"g_pv{j}"), t + 1)
                    if j == 0:
                        if past(32 * t):
                            dve.wait_ge(sem("st_done"), 32 * t)
                        if past(t):
                            dve.wait_ge(sem("g_hT1"), t)
                    last = v.tensor_tensor(mix[:, 256 * j:256 * j + 256].rearrange("p (a b) -> p a b", a=G),
                                    b7[:, 256 * j:256 * j + 256].rearrange("p (a b) -> p a b", a=G),
                                    bc(at4[:, 4, :], [P, G, HD]), ALU.mult)
                    if j:
                        last.then_inc(sem("att1"), 1)
                return f

            def inter(t, p):
                C = C_s if isinstance(t, int) and t == SAMPLE else C_p
                dve.wait_ge(sem("g_intra"), t + 1)
                dve.wait_ge(sem("c_inter"), t + 1)
                for i in range(2):
                    part = num[:, 2 * i:2 * i + 2, :]
                    last = v.tensor_tensor(part, b56[:, 512 * i:512 * i + 2 * (MD + 1)].rearrange("p (a b) -> p a b", a=2), part, ALU.add)
                last.then_inc(sem("c_num"), 1)

            def delta(t, p):
                C = C_s if isinstance(t, int) and t == SAMPLE else C_p
                dve.wait_ge(sem("g_delta"), t + 1)
                for h in range(MH):
                    last = v.scalar_tensor_tensor(out=C[:, h, :], in0=C[:, h, :], scalar=dec[:, h:h + 1], in1=head2(b56, h),
                                                  op0=ALU.mult, op1=ALU.add)
                last.then_inc(sem("c_delta"), 1)
                if isinstance(t, int) and t in (NPT - 1, SAMPLE):
                    dve.wait_ge(sem("g_stout"), 1 + (t == SAMPLE))
                    if t == SAMPLE:
                        dve.wait_ge(sem("state_out"), 48)
                    v.tensor_copy(kw[:], b56[:, 0:512].rearrange("p (a b) -> p a b", a=MH)).then_inc(sem("state_ok"), 1)

            def mid(t, p):
                dve.wait_ge(sem("c_num"), t + 1)
                st(v.scalar_tensor_tensor(out=ml4[:, 0, :], in0=num[:, :, MD], scalar=-1.0, in1=num[:, :, MD],
                                          op0=ALU.mult, op1=ALU.max))
                st(v.tensor_tensor(ml4[:, 0, :], ml4[:, 0, :], cols[:, 96:96 + MH], ALU.max))
                st(v.reciprocal(ml4[:, 0, :], ml4[:, 0, :]))
                st(v.tensor_tensor(ml4[:, 1, :], ml4[:, 0, :], ml4[:, 0, :], ALU.mult))
                dve.wait_ge(sem("h_sq"), t + 1)
                v.tensor_tensor(ml4[:, 3, :], ml4[:, 1, :], ml4[:, 2, :], ALU.mult).then_inc(sem("h_ms"), 1)
                dve.wait_ge(sem("o_sig"), t + 1)
                v.tensor_tensor(og[:], og[:], g_mh[:], ALU.mult)
                dve.wait_ge(sem("h_rs"), t + 1)
                st(v.tensor_tensor(ml4[:, 6, :], ml4[:, 5, :], ml4[:, 0, :], ALU.mult))
                st(v.tensor_tensor(wT[:], num[:, :, 0:MD], bc(ml4[:, 6, :], [P, MH, MD]), ALU.mult))
                if past(32 * t):
                    dve.wait_ge(sem("st_done"), 32 * t)
                v.tensor_tensor(mix[:, 512:1024].rearrange("p (a b) -> p a b", a=MH), wT[:], og[:], ALU.mult).then_inc(sem("mixed_h"), 1)

            def out_gate(t, p):
                dve.wait_ge(sem("c_o"), t + 1)
                v.tensor_scalar(og[:], og[:], 1e18, 1.0, ALU.min, ALU.add).then_inc(sem("o_1e"), 1)

            def proj(t, p):
                sample = isinstance(t, int) and t == SAMPLE
                dve.wait_ge(sem("rows_in"), 16 * (6 if sample else 3))
                dve.wait_ge(sem("xr_in"), 16 * (t + 1))
                dve.wait_ge(sem("g_mx1"), t + 1)
                for i, bank in ((0, b1), (1, b2)):
                    h = slice(512 * i, 512 * i + 512)
                    dve.wait_ge(sem(f"g_pr{i}"), t + 1)
                    st(v.tensor_tensor(mix[:, h], bank[:], row_gate[:, h], ALU.mult))
                    last = v.tensor_tensor(xr[:, h], xr[:, h], mix[:, h], ALU.add)
                last.then_inc(sem("x1_ok"), 1)
                dve.wait_ge(sem("rstd2"), t + 1)
                st(v.scalar_tensor_tensor(out=mix[:], in0=xr[:], scalar=nr[:, 6:7], in1=row_g2[:], op0=ALU.mult, op1=ALU.mult))
                v.tensor_tensor(mix[:], mix[:], row_s2[:], ALU.add).then_inc(sem("h2"), 1)

            def route(t, p):
                sample = isinstance(t, int) and t == SAMPLE
                io4, io32 = iotas[:, 0:NG], iotas[:, NG:NG + NE]
                dve.wait_ge(sem("g_lg"), t + 1)
                v.tensor_tensor(lg8[:, 0:NG], b2[:, 0:NG], b_r[:, 0:NG], ALU.add)
                st(v.tensor_tensor(le[:], b2[:, NG:NG + NE], b_r[:, NG:NG + NE], ALU.add))
                apart(dve)
                st(v.max(gm8[:], lg8[:]))
                v.tensor_scalar(rc[:, 0:1], gm8[:, 0:1], -1.0, None, ALU.mult).then_inc(sem("g_max"), 1)
                st(v.max_index(gi8[:], gm8[:], lg8[:]))
                st(v.tensor_copy(rc[:, 2:3], gi8[:, 0:1]))
                st(v.tensor_scalar(gmk[:, 0, :], io4, rc[:, 2:3], None, ALU.is_equal))
                st(v.tensor_scalar(gmk[:, 1, :], gmk[:, 0, :], -1.0, BIG, ALU.add, ALU.mult))
                l3 = le[:].rearrange("p (a b) -> p a b", a=NG)
                st(v.tensor_tensor(l3, l3, bc(gmk[:, 0, :], [P, NG, EPG]), ALU.mult))
                st(v.tensor_tensor(l3, l3, bc(gmk[:, 1, :], [P, NG, EPG]), ALU.add))
                apart(dve)
                st(v.max(lv8[:], le[:]))
                v.tensor_tensor(rc[:, 9:10], lv8[:, 1:2], lv8[:, 0:1], ALU.subtract).then_inc(sem("e_dif"), 1)
                st(v.max_index(li8[:], lv8[:], le[:]))
                st(v.tensor_copy(rc[:, 2:4], li8[:, 0:2]))
                v.tensor_scalar(oh[:, 0, :], io32, rc[:, 2:3], None, ALU.is_equal)
                st(v.tensor_scalar(oh[:, 1, :], io32, rc[:, 3:4], None, ALU.is_equal))
                m = v.tensor_tensor(oh[:, 2, :], oh[:, 0, :], oh[:, 1, :], ALU.add)
                if sample:
                    st(m)
                    m = v.tensor_scalar(oh[:, 2, :], oh[:, 2, :], padcol[:, 0:1], None, ALU.mult)
                m.then_inc(sem("M_ok"), 1)

            def rank(t, p):
                dve.wait_ge(sem("g_rank"), t + 1)
                v.tensor_tensor(Msum[:], Msum[:], oh[:, 2, :], ALU.add)
                v.tensor_tensor(oh[:, 3, :], b2[:, 64:64 + NE], iotas[:, NG + NE:], ALU.add).then_inc(sem("c_rank"), 1)

            def slots(t, p):
                sample = isinstance(t, int) and t == SAMPLE
                dve.wait_ge(sem("g_exp"), t + 1)
                dve.wait_ge(sem("e_exp"), t + 1)
                st(v.tensor_scalar(rc[:, 11:12], rc[:, 10:11], 1.0, None, ALU.add))
                st(v.tensor_tensor(rc[:, 11:12], rc[:, 11:12], rc[:, 1:2], ALU.mult))
                st(v.reciprocal(rc[:, 12:13], rc[:, 11:12]))
                v.tensor_copy(gate_all[:, 0, one(t)], rc[:, 12:13])
                v.tensor_tensor(gate_all[:, 1, one(t)], rc[:, 12:13], rc[:, 10:11], ALU.mult)
                dve.wait_ge(sem("c_rank"), t + 1)
                for k in range(2):
                    st(v.tensor_tensor(oh[:, 4, :], oh[:, 3, :], oh[:, k, :], ALU.mult))
                    st(v.tensor_reduce(rc[:, 13 + k:14 + k], oh[:, 4, :], AX.X, ALU.add))
                if sample:
                    st(v.scalar_tensor_tensor(out=rc[:, 13:15], in0=rc[:, 13:15], scalar=padcol[:, 0:1], in1=padcol[:, 1:3],
                                              op0=ALU.mult, op1=ALU.add))
                if past(32 * t):
                    dve.wait_ge(sem("scat"), 32 * t)
                v.tensor_copy(dst[:], rc[:, 13:15]).then_inc(sem("dst_ok"), 1)

            def turn(t, p):
                if has(t - 1):
                    qk(t - 1, 1 - p)
                    columns(t - 1, 1 - p)
                if has(t - 2):
                    rank(t - 2, p)
                if has(t - 1):
                    weights(t - 1, 1 - p)
                    softmax(0)(t - 1, 1 - p)
                    weights2(t - 1, 1 - p)
                if has(t - 2):
                    slots(t - 2, p)
                if has(t - 1):
                    turned(0)(t - 1, 1 - p)
                    attend(0)(t - 1, 1 - p)
                    inter(t - 1, 1 - p)
                if has(t):
                    gates_evac(t, p)
                if has(t - 1):
                    softmax(1)(t - 1, 1 - p)
                    delta(t - 1, 1 - p)
                    mid(t - 1, 1 - p)
                    turned(1)(t - 1, 1 - p)
                    attend(1)(t - 1, 1 - p)
                if has(t):
                    prep(t, p)
                    gate(t, p)
                if has(t - 1):
                    proj(t - 1, 1 - p)
                if has(t):
                    silu(t, p)
                if has(t - 1):
                    route(t - 1, 1 - p)
                if has(t):
                    out_gate(t, p)

            walk(dve, turn, st, STEPS["dve"])

            dve.wait_ge(sem("g_cnt"), 1)
            st(v.tensor_scalar(cnt_f[:, 0, :], b2[0:1, 0:NE], P - 1.0, None, ALU.add))
            st(v.tensor_copy(cnt_i[:, 0, :], cnt_f[:, 0, :]))
            st(v.tensor_scalar(cnt_i[:, 0, :], cnt_i[:, 0, :], 7, None, ALU.arith_shift_right))
            st(v.tensor_copy(cnt_f[:, 0, :], cnt_i[:, 0, :]))
            st(v.tensor_scalar(cnt_f[:, 0, :], cnt_f[:, 0, :], 1.0, None, ALU.max))
            st(v.tensor_tensor_scan(cnt_f[:, 1, :], ones[0:1, 0:NE], cnt_f[:, 0, :], 0.0, ALU.mult, ALU.add))
            st(v.tensor_tensor(cnt_f[:, 2, :], cnt_f[:, 1, :], cnt_f[:, 0, :], ALU.subtract))
            v.tensor_copy(cnt_i[:, 0, :], cnt_f[:, 0, :])
            v.tensor_copy(cnt_i[:, 2, :], cnt_f[:, 1, NE - 1:NE].broadcast_to([1, NE]))
            v.tensor_copy(cnt_i[:, 1, :], cnt_f[:, 2, :]).then_inc(sem("cnt_ok"), 1)
            dve.wait_ge(sem("st_done"), 32 * NT)
            v.memset(yrow[:], 0.0).then_inc(sem("ye"), 1)
            dve.wait_ge(sem("g_lists"), 1)
            st(v.tensor_copy(sidx_all, b34[:, 0:NB]))
            st(v.tensor_scalar(smf[:, 0:NB], b34[:, 0:NB], float(NT * P), -float(NT * P), ALU.is_ge, ALU.mult))
            st(v.tensor_tensor(smf[:, 0:NB], b34[:, 0:NB], smf[:, 0:NB], ALU.add))
            st(v.tensor_scalar(num_f, smf[:, 0:NB], float(NT * P), -float(NT * P), ALU.is_ge, ALU.mult))
            dve.wait_ge(sem("rstd2"), NT)
            v.tensor_tensor(idx_all, smf[:, 0:NB], num_f, ALU.add).then_inc(sem("idx_ok"), 1)
            dve.wait_ge(sem("cnt_ok"), 1)

            def rows_in(g):
                dve.wait_ge(sem("g_x"), g + 2)
                for i, bank in ((0, b0), (1, b1)):
                    last = v.tensor_copy(xT[:, 4 * i:4 * i + 4, :], bank[:].rearrange("p (a b) -> p a b", a=4))
                last.then_inc(sem("c_x"), 1)

            rows_in(0)
            with dve.Fori(0, NE) as e:
                n = dve.value_load(cnt_i[0:1, 0, bass.ds(e, 1)], min_val=1, max_val=CAP)
                g0 = dve.value_load(cnt_i[0:1, 1, bass.ds(e, 1)], min_val=0, max_val=NB)
                with dve.Fori(0, n) as b:
                    g = g0 + b
                    dve.wait_ge(sem("gu"), 2 * g + 2)
                    dve.wait_ge(sem("ge"), g + 1)
                    for half in (slice(0, FE // 2), slice(FE // 2, FE)):
                        v.tensor_tensor(e_a[:, half], b7[:, half], e_a[:, half], ALU.mult).then_inc(sem("a_ok"), 1)
                    dve.wait_ge(sem("g_aT"), 2 * g + 2)
                    v.tensor_copy(aT[:, 2:4, :], b34[:, 512:768].rearrange("p (a b) -> p a b", a=2)).then_inc(sem("c_a1"), 1)
                    rows_in(g + 1)

            dve.wait_ge(sem("rows4_in"), 48)

            def combine(t, k, turn, n=P):
                r0, r1, x1, out = (z[0:n, :] for z in f_r[k])
                gate5 = row_s2 if isinstance(t, int) and t == SAMPLE else row_gate
                dve.wait_ge(sem(f"x1_in{k}"), 48 * (turn + 1))
                dve.wait_ge(sem("f_r0"), t + 1)
                st(v.scalar_tensor_tensor(out=r0, in0=r1, scalar=f_g[k][0:n, 1:2], in1=r0, op0=ALU.mult, op1=ALU.add))
                st(v.tensor_tensor(r0, r0, gate5[0:n, :], ALU.mult))
                v.tensor_tensor(x1, x1, r0, ALU.add).then_inc(sem("f_x"), 1)

            def last_scale(t, k, n=P):
                dve.wait_ge(sem("f_rs"), t + 1)
                v.scalar_tensor_tensor(out=f_r[k][3][0:n, :], in0=f_r[k][2][0:n, :], scalar=nr[0:n, k + 2:k + 3],
                                       in1=row_g2[0:n, :], op0=ALU.mult, op1=ALU.mult).then_inc(sem("y_ok"), 1)

            def last_tiles(t, turn):
                for k in range(NB4):
                    combine(t + k, k, turn)
                    if k or not (isinstance(t, int) and t == 0):
                        last_scale(t + k - 1, (k - 1) % NB4)

            start = st.n
            last_tiles(0, 0)
            with dve.Fori(1, NPT // NB4) as i:
                st.base, st.n = 2 * NB4 * (i - 1), start + 2 * NB4
                last_tiles(NB4 * i, i)
            st.base, st.n = 0, start + 2 * NPT
            combine(SAMPLE, 0, NPT // NB4, DEC)
            last_scale(SAMPLE - 1, NB4 - 1)
            last_scale(SAMPLE, 0, DEC)


_INS = ["x", "c_both", "w_ada", "b_ada", "g_mix", "g_ffn", "w_in", "sinks", "taps", "b_ig", "b_fg", "g_mh", "w_out",
        "w_r", "b_r", "w_g", "w_u", "w_d", "g_final", "cache_k", "cache_v", "state_conv", "state_C", "state_n",
        "state_m", "c_ident", "c_cmask", "c_lower", "c_amask", "c_iotas", "c_tokid", "c_padcol", "c_trash", "rope"]


def kernel(**inp):
    import numpy as np
    import concourse.bacc as bacc
    from concourse.bass_utils import run_bass_kernel_spmd

    f = np.float32
    inp = {k: np.ascontiguousarray(v) for k, v in inp.items()}
    a = {}
    a["x"] = np.concatenate([inp["x_prompt"][0], inp["x_sample"][0], np.zeros((P - DEC, D), f)])
    a["c_both"] = np.stack([inp["c_prompt"][0], inp["c_sample"][0]], axis=1)
    a["w_ada"], a["b_ada"] = inp["w_ada"][0], inp["b_ada"][0]
    a["g_mix"], a["g_ffn"], a["g_final"] = inp["g_norm_mix"][0], inp["g_norm_ffn"][0], inp["g_final"]
    order = np.concatenate([np.arange(NH * HD).reshape(NKV, G, HD).transpose(1, 0, 2).ravel(), np.arange(NH * HD, inp["w_in"].shape[2])])
    a["w_in"] = inp["w_in"][0][:, order]
    a["w_in"] = np.insert(a["w_in"], [I0 + MH] * (32 - MH), 0.0, axis=1)
    a["sinks"], a["b_ig"], a["b_fg"] = inp["attn_sinks"][0], inp["b_igate"][0], inp["b_fgate"][0]
    a["taps"] = np.concatenate([inp["conv_w"][0], inp["conv_b"]]).reshape(CW + 1, KT, P).transpose(2, 0, 1)
    a["g_mh"], a["w_out"] = inp["g_mhnorm"][0], inp["w_out"][0]
    a["w_r"] = np.concatenate([inp["w_router_group"][0], inp["w_router_expert"][0]], axis=1)
    a["b_r"] = np.concatenate([inp["b_router_group"][0], inp["b_router_expert"][0]])
    a["w_g"], a["w_u"], a["w_d"] = inp["w_exp_gate"][0], inp["w_exp_up"][0], inp["w_exp_down"][0]
    a["cache_k"] = inp["cache_win_k"].reshape(P, NKV * HD)
    a["cache_v"] = inp["cache_win_v"].reshape(P, NKV * HD)
    a["state_conv"] = inp["state_conv"].reshape(CW - 1, KT, P).transpose(2, 0, 1)
    a["state_C"], a["state_n"], a["state_m"] = inp["state_C"][0, 0], inp["state_n"][0, 0], inp["state_m"][0, 0]
    i = np.arange(P)
    a["c_ident"] = np.eye(P, dtype=f)
    a["c_cmask"] = np.where(i[:, None] <= i[None, :], 0.0, -BIG).astype(f)
    a["c_lower"] = (i[:, None] < i[None, :]).astype(f)
    key = np.arange(2 * P)[None, :]
    q = i[:, None]
    band = (key // CHUNK >= q // CHUNK) & (key // CHUNK <= q // CHUNK + 2)
    a["c_amask"] = np.stack([np.where(m, 0.0, -BIG) for m in
                             (band & (key >= P), band, np.broadcast_to(key < P + DEC, band.shape))], axis=1).astype(f)
    a["c_iotas"] = np.tile(np.concatenate([np.arange(NG), np.arange(NE), np.arange(NE) * CAP * P]), (P, 1)).astype(f)
    a["c_tokid"] = (i[:, None] + P * np.arange(NT)[None, :]).astype(f)
    a["c_trash"] = np.tile(TRASH + i, (P, 1)).astype(f)
    pad = (i >= DEC).astype(f)
    a["c_padcol"] = np.stack([1 - pad, pad * (SLOTS + i), pad * (SLOTS + P + i)], axis=1).astype(f)
    pos = np.concatenate([np.arange(SEQ), PAST + np.arange(P)]).astype(f)
    freq = (f(500000.0) ** (-np.arange(0, ROT, 2, dtype=f) / f(ROT))).astype(f)
    ang = pos[:, None] * freq[None, :]
    c, s = np.cos(ang), np.sin(ang)
    a["rope"] = np.concatenate([c, c, -s, s], axis=1).astype(f)

    nc = bacc.Bacc("TRN2", target_bir_lowering=False, num_devices=1)
    arrays, ins, outs = {}, {}, {}
    for name in _INS:
        arrays[f"in_{name}"] = np.ascontiguousarray(a[name])
        ins[name] = nc.dram_tensor(f"in_{name}", arrays[f"in_{name}"].shape, F32, kind="ExternalInput").ap()
    shapes = {"y_p": (SEQ, D), "y_s": (DEC, D)}
    for s_ in "ps":
        shapes |= {f"k_{s_}": (P, NKV * HD), f"v_{s_}": (P, NKV * HD), f"conv_{s_}": (P, CW - 1, KT),
                   f"C_{s_}": (MH, MD, MD), f"n_{s_}": (MH, MD), f"m_{s_}": (MH,)}
    for name, shape in shapes.items():
        outs[name] = nc.dram_tensor(f"out_{name}", shape, F32, kind="ExternalOutput").ap()
    build(nc, ins, outs)
    r = run_bass_kernel_spmd(nc, [arrays], core_ids=[0]).results[0]
    got = {name: r[f"out_{name}"] for name in shapes}
    res = [got["y_p"].reshape(1, SEQ, D), got["y_s"].reshape(1, DEC, D)]
    for s_ in "ps":
        res += [got[f"k_{s_}"].reshape(1, 1, P, NKV, HD), got[f"v_{s_}"].reshape(1, 1, P, NKV, HD),
                got[f"conv_{s_}"].transpose(1, 2, 0).reshape(1, 1, CW - 1, 2 * MH * MD),
                got[f"C_{s_}"].reshape(1, 1, MH, MD, MD), got[f"n_{s_}"].reshape(1, 1, MH, MD), got[f"m_{s_}"].reshape(1, 1, MH)]
    return tuple(res)
```
